# Optimizing a Trainium2 kernel written in Bass

```python
import math
import jax, jax.numpy as jnp
from jax import lax
import numpy as np

D_MODEL = 1024
BATCH = 1
SEQ = 256
DEPTH = 1
DEC_BATCH = 8
DEC_SEQ = 16
PAST_LEN = 256

CHUNK = 64
S5_WIDTH = 512
S5_GROUP = 16
S5_GROUPS = S5_WIDTH // S5_GROUP
S5_STATE = 64
RET_HEADS = 4
RET_DK = 128
RET_DV = 256
RET_QK = RET_HEADS * RET_DK
RET_V = RET_HEADS * RET_DV
ROPE_BASE = 10000.0
MOE_GROUPS = 4
MOE_EXPERTS = 8
MOE_TOPK = 2
MOE_FF = 256
EPS = 1e-6
IN_SPLITS = (S5_WIDTH, RET_QK, RET_QK, RET_V, RET_V, D_MODEL, D_MODEL)
IN_WIDTH = S5_WIDTH + 2 * RET_QK + 2 * RET_V + 2 * D_MODEL

kernel_name = 'hybrid_s5_retention_hmoe_stream_step'

def rmsnorm(x, g):
    xf = x.astype(jnp.float32)
    y = xf * lax.rsqrt(jnp.mean(xf * xf, axis=-1, keepdims=True) + EPS)
    return (y * g.astype(jnp.float32)).astype(x.dtype)

def modulate(n, shift, scale):
    return n * (1.0 + scale[:, None, :]) + shift[:, None, :]

def s5_discretise(a_re, a_im, log_dt, b_re, b_im):
    f32 = jnp.float32
    a_re = a_re.astype(f32)
    a_im = a_im.astype(f32)
    dt = jnp.exp(log_dt.astype(f32))[:, None]
    mag = jnp.exp(a_re * dt)
    ang = a_im * dt
    ab_re = mag * jnp.cos(ang)
    ab_im = mag * jnp.sin(ang)
    den = a_re * a_re + a_im * a_im
    nr = ab_re - 1.0
    ni = ab_im
    f_re = (nr * a_re + ni * a_im) / den
    f_im = (ni * a_re - nr * a_im) / den
    b_re = b_re.astype(f32)
    b_im = b_im.astype(f32)
    bb_re = f_re[..., None] * b_re - f_im[..., None] * b_im
    bb_im = f_re[..., None] * b_im + f_im[..., None] * b_re
    return ab_re, ab_im, bb_re, bb_im

def _ssm_combine(e1, e2):
    ar1, ai1, br1, bi1 = e1
    ar2, ai2, br2, bi2 = e2
    ar = ar1 * ar2 - ai1 * ai2
    ai = ar1 * ai2 + ai1 * ar2
    br = ar2 * br1 - ai2 * bi1 + br2
    bi = ar2 * bi1 + ai2 * br1 + bi2
    return (ar, ai, br, bi)

def s5_mixer(u, h0_re, h0_im, a_re, a_im, log_dt, b_re, b_im, c_re, c_im, d_skip, w_glu, b_glu):
    f32 = jnp.float32
    bsz, seq_len, _ = u.shape
    uf = u.astype(f32).reshape(bsz, seq_len, S5_GROUPS, S5_GROUP)
    ab_re, ab_im, bb_re, bb_im = s5_discretise(a_re, a_im, log_dt, b_re, b_im)
    bu_re = jnp.einsum('blgj,gpj->blgp', uf, bb_re)
    bu_im = jnp.einsum('blgj,gpj->blgp', uf, bb_im)
    shape = bu_re.shape
    elems = (jnp.broadcast_to(ab_re, shape), jnp.broadcast_to(ab_im, shape), bu_re, bu_im)
    ap_re, ap_im, x_re, x_im = lax.associative_scan(_ssm_combine, elems, axis=1)
    if h0_re is not None:
        h_re = h0_re.astype(f32)[:, None]
        h_im = h0_im.astype(f32)[:, None]
        x_re, x_im = (x_re + ap_re * h_re - ap_im * h_im,
                      x_im + ap_re * h_im + ap_im * h_re)
    y = (jnp.einsum('blgp,gjp->blgj', x_re, c_re.astype(f32))
         - jnp.einsum('blgp,gjp->blgj', x_im, c_im.astype(f32))
         + d_skip.astype(f32).reshape(S5_GROUPS, S5_GROUP) * uf)
    y = y.reshape(bsz, seq_len, S5_WIDTH)
    z = jax.nn.gelu(y)
    out = z * jax.nn.sigmoid(z @ w_glu.astype(f32) + b_glu.astype(f32))
    return out, x_re[:, -1], x_im[:, -1]

def rotary(x, pos):
    half = RET_DK // 2
    theta = 1.0 / (ROPE_BASE ** jnp.linspace(0.0, 1.0, half, dtype=jnp.float32))
    ang = pos.astype(jnp.float32)[:, None] * theta[None, :]
    cos = jnp.cos(ang)[None, :, None, :]
    sin = jnp.sin(ang)[None, :, None, :]
    x1 = x[..., :half]
    x2 = x[..., half:]
    return jnp.concatenate([x1 * cos - x2 * sin, x1 * sin + x2 * cos], axis=-1)

def retention_mixer(q, k, v, s0, offset):
    f32 = jnp.float32
    bsz, seq_len, _ = q.shape
    cl = min(CHUNK, seq_len)
    nc = seq_len // cl
    pos = offset + jnp.arange(seq_len)
    qh = rotary(q.astype(f32).reshape(bsz, seq_len, RET_HEADS, RET_DK), pos)
    kh = rotary(k.astype(f32).reshape(bsz, seq_len, RET_HEADS, RET_DK), pos) * (RET_DK ** -0.5)
    vh = v.astype(f32).reshape(bsz, seq_len, RET_HEADS, RET_DV)
    log_g = jnp.log(1.0 - 2.0 ** (-5.0 - jnp.arange(RET_HEADS, dtype=f32)))
    idx = jnp.arange(cl, dtype=f32)
    inner_decay = jnp.exp(log_g[:, None, None] * jnp.abs(idx[:, None] - idx[None, :]))
    qc = qh.reshape(bsz, nc, cl, RET_HEADS, RET_DK)
    kc = kh.reshape(bsz, nc, cl, RET_HEADS, RET_DK)
    vc = vh.reshape(bsz, nc, cl, RET_HEADS, RET_DV)
    scores = jnp.einsum('bnchd,bnmhd->bnhcm', qc, kc) * inner_decay
    inner = jnp.einsum('bnhcm,bnmhe->bnche', scores, vc)
    zeta = jnp.exp(log_g[:, None] * (cl - 1.0 - idx)[None, :])
    kv = jnp.einsum('bnmhd,bnmhe,hm->nbhde', kc, vc, zeta)
    chunk_decay = jnp.exp(log_g * cl)[None, :, None, None]
    init = jnp.zeros((bsz, RET_HEADS, RET_DK, RET_DV), f32) if s0 is None else s0.astype(f32)

    def step(s, kv_n):
        return chunk_decay * s + kv_n, s

    s_last, s_prev = lax.scan(step, init, kv)
    xi = jnp.exp(log_g[:, None] * (idx + 1.0)[None, :])
    cross = jnp.einsum('bnchd,nbhde,hc->bnche', qc, s_prev, xi)
    o = (inner + cross).reshape(bsz, seq_len, RET_HEADS, RET_DV)
    o = o * lax.rsqrt(jnp.mean(o * o, axis=-1, keepdims=True) + EPS)
    return o.reshape(bsz, seq_len, RET_V), s_last

def hmoe(x, w_rg, b_rg, w_re, b_re, w1, w3, w2):
    f32 = jnp.float32
    bsz, seq_len, dm = x.shape
    t = x.reshape(bsz * seq_len, dm)
    tf = t.astype(f32)
    g_logits = tf @ w_rg.astype(f32) + b_rg.astype(f32)
    g_prob = jax.nn.softmax(g_logits, axis=-1)
    _, g_idx = lax.top_k(g_logits, 1)
    g_w = jnp.take_along_axis(g_prob, g_idx, axis=-1)
    g_onehot = jax.nn.one_hot(g_idx[:, 0], MOE_GROUPS, dtype=f32)
    e_all = jnp.einsum('td,gde->tge', tf, w_re.astype(f32)) + b_re.astype(f32)
    e_logits = jnp.einsum('tge,tg->te', e_all, g_onehot)
    e_top, e_idx = lax.top_k(e_logits, MOE_TOPK)
    e_w = jax.nn.softmax(e_top, axis=-1)
    e_dense = jnp.einsum('tk,tke->te', e_w, jax.nn.one_hot(e_idx, MOE_EXPERTS, dtype=f32))
    gate = (g_w * g_onehot)[:, :, None] * e_dense[:, None, :]
    out = jnp.zeros((bsz * seq_len, dm), f32)
    for gi in range(MOE_GROUPS):
        h = jax.nn.silu(jnp.einsum('td,edf->tef', t, w1[gi])) * jnp.einsum('td,edf->tef', t, w3[gi])
        out = out + jnp.einsum('tef,efd->td', h * gate[:, gi, :, None].astype(h.dtype), w2[gi])
    return out.reshape(bsz, seq_len, dm)

def trunk_layer(x, c, s5_re0, s5_im0, ret0, offset, p):
    mod = jax.nn.silu(c) @ p['w_ada'] + p['b_ada']
    sh1, sc1, gt1, sh2, sc2, gt2 = jnp.split(mod, 6, axis=-1)
    n = modulate(rmsnorm(x, p['norm1']), sh1, sc1)
    proj = n @ p['w_in']
    offsets = np.cumsum(IN_SPLITS)[:-1].tolist()
    u, q, k, v, g, gate_a, gate_b = jnp.split(proj, offsets, axis=-1)
    y_a, s5_re, s5_im = s5_mixer(u, s5_re0, s5_im0, p['s5_a_re'], p['s5_a_im'], p['s5_log_dt'],
                                 p['s5_b_re'], p['s5_b_im'], p['s5_c_re'], p['s5_c_im'],
                                 p['s5_d'], p['s5_w_glu'], p['s5_b_glu'])
    y_b, ret_s = retention_mixer(q, k, v, ret0, offset)
    y_a = y_a @ p['w_s5_out']
    y_b = (y_b * jax.nn.silu(g)) @ p['w_ret_out']
    merged = jax.nn.sigmoid(gate_a) * y_a + jax.nn.sigmoid(gate_b) * y_b
    x = x + gt1[:, None, :] * (merged @ p['w_out'])
    n2 = modulate(rmsnorm(x, p['norm2']), sh2, sc2)
    x = x + gt2[:, None, :] * hmoe(n2, p['w_rg'], p['b_rg'], p['w_re'], p['b_re'],
                                   p['w1'], p['w3'], p['w2'])
    return x, s5_re, s5_im, ret_s

def setup_inputs(seed: int = 0) -> dict:
    key = jax.random.key(seed)
    ks = jax.random.split(key, 40)
    f32 = jnp.float32

    def nrm(i, shape, scale):
        return scale * jax.random.normal(ks[i], shape, f32)

    G, P, J = S5_GROUPS, S5_STATE, S5_GROUP
    a_im_base = jnp.pi * jnp.arange(P, dtype=f32)
    return {
        'x_prompt': nrm(0, (BATCH, SEQ, D_MODEL), 1.0),
        'x_sample': nrm(1, (DEC_BATCH, DEC_SEQ, D_MODEL), 1.0),
        'state_s5_re': nrm(2, (DEPTH, DEC_BATCH, G, P), 0.3),
        'state_s5_im': nrm(3, (DEPTH, DEC_BATCH, G, P), 0.3),
        'state_ret': nrm(4, (DEPTH, DEC_BATCH, RET_HEADS, RET_DK, RET_DV), 1.0),
        'c_prompt': nrm(5, (BATCH, D_MODEL), 1.0),
        'c_sample': nrm(6, (DEC_BATCH, D_MODEL), 1.0),
        'w_ada': nrm(7, (DEPTH, D_MODEL, 6 * D_MODEL), 0.5 * D_MODEL ** -0.5),
        'b_ada': nrm(8, (DEPTH, 6 * D_MODEL), 0.02),
        'norm1': 1.0 + nrm(9, (DEPTH, D_MODEL), 0.02),
        'norm2': 1.0 + nrm(10, (DEPTH, D_MODEL), 0.02),
        'w_in': nrm(11, (DEPTH, D_MODEL, IN_WIDTH), D_MODEL ** -0.5),
        's5_a_re': -0.5 + nrm(12, (DEPTH, G, P), 0.01),
        's5_a_im': a_im_base + nrm(13, (DEPTH, G, P), 0.01),
        's5_log_dt': jax.random.uniform(ks[14], (DEPTH, G), f32, math.log(0.001), math.log(0.1)),
        's5_b_re': nrm(15, (DEPTH, G, P, J), (2.0 * J) ** -0.5),
        's5_b_im': nrm(16, (DEPTH, G, P, J), (2.0 * J) ** -0.5),
        's5_c_re': nrm(17, (DEPTH, G, J, P), P ** -0.5),
        's5_c_im': nrm(18, (DEPTH, G, J, P), P ** -0.5),
        's5_d': nrm(19, (DEPTH, S5_WIDTH), 0.5),
        's5_w_glu': nrm(20, (DEPTH, S5_WIDTH, S5_WIDTH), S5_WIDTH ** -0.5),
        's5_b_glu': nrm(21, (DEPTH, S5_WIDTH), 0.02),
        'w_s5_out': nrm(22, (DEPTH, S5_WIDTH, D_MODEL), S5_WIDTH ** -0.5),
        'w_ret_out': nrm(23, (DEPTH, RET_V, D_MODEL), RET_V ** -0.5),
        'w_out': nrm(24, (DEPTH, D_MODEL, D_MODEL), D_MODEL ** -0.5),
        'w_rg': nrm(25, (DEPTH, D_MODEL, MOE_GROUPS), D_MODEL ** -0.5),
        'b_rg': nrm(26, (DEPTH, MOE_GROUPS), 0.01),
        'w_re': nrm(27, (DEPTH, MOE_GROUPS, D_MODEL, MOE_EXPERTS), D_MODEL ** -0.5),
        'b_re': nrm(28, (DEPTH, MOE_GROUPS, MOE_EXPERTS), 0.01),
        'w1': nrm(29, (DEPTH, MOE_GROUPS, MOE_EXPERTS, D_MODEL, MOE_FF), D_MODEL ** -0.5),
        'w3': nrm(30, (DEPTH, MOE_GROUPS, MOE_EXPERTS, D_MODEL, MOE_FF), D_MODEL ** -0.5),
        'w2': nrm(31, (DEPTH, MOE_GROUPS, MOE_EXPERTS, MOE_FF, D_MODEL), MOE_FF ** -0.5),
        'final_norm': 1.0 + nrm(32, (D_MODEL,), 0.02),
    }

def reference(x_prompt, x_sample, state_s5_re, state_s5_im, state_ret, c_prompt, c_sample,
              w_ada, b_ada, norm1, norm2, w_in, s5_a_re, s5_a_im, s5_log_dt, s5_b_re, s5_b_im,
              s5_c_re, s5_c_im, s5_d, s5_w_glu, s5_b_glu, w_s5_out, w_ret_out, w_out,
              w_rg, b_rg, w_re, b_re, w1, w3, w2, final_norm):
    hp = x_prompt
    hs = x_sample
    p_re, p_im, p_ret = [], [], []
    s_re, s_im, s_ret = [], [], []
    for l in range(DEPTH):
        p = dict(w_ada=w_ada[l], b_ada=b_ada[l], norm1=norm1[l], norm2=norm2[l], w_in=w_in[l],
                 s5_a_re=s5_a_re[l], s5_a_im=s5_a_im[l], s5_log_dt=s5_log_dt[l],
                 s5_b_re=s5_b_re[l], s5_b_im=s5_b_im[l], s5_c_re=s5_c_re[l], s5_c_im=s5_c_im[l],
                 s5_d=s5_d[l], s5_w_glu=s5_w_glu[l], s5_b_glu=s5_b_glu[l],
                 w_s5_out=w_s5_out[l], w_ret_out=w_ret_out[l], w_out=w_out[l],
                 w_rg=w_rg[l], b_rg=b_rg[l], w_re=w_re[l], b_re=b_re[l],
                 w1=w1[l], w3=w3[l], w2=w2[l])
        hp, r_re, r_im, r_ret = trunk_layer(hp, c_prompt, None, None, None, 0, p)
        hs, q_re, q_im, q_ret = trunk_layer(hs, c_sample, state_s5_re[l], state_s5_im[l],
                                            state_ret[l], PAST_LEN, p)
        p_re.append(r_re)
        p_im.append(r_im)
        p_ret.append(r_ret)
        s_re.append(q_re)
        s_im.append(q_im)
        s_ret.append(q_ret)
    y_prompt = rmsnorm(hp, final_norm)
    y_sample = rmsnorm(hs, final_norm)
    return (y_prompt, y_sample, jnp.stack(p_re), jnp.stack(p_im), jnp.stack(p_ret),
            jnp.stack(s_re), jnp.stack(s_im), jnp.stack(s_ret))


_drawn_inputs = setup_inputs


def setup_inputs(seed=0):
    import zlib

    import numpy as np

    out = dict(_drawn_inputs(seed))
    spreads = {}
    factors = {'norm2': 4.03,
     's5_a_re': 4.027,
     's5_c_re': 3.302,
     's5_c_im': 3.301,
     's5_w_glu': 4.874,
     's5_b_glu': 8.0,
     'b_rg': 8.0,
     'b_re': 8.0,
     'final_norm': 2.737}
    for name, (base, spread) in spreads.items():
        noise = np.random.default_rng([zlib.crc32(name.encode()), seed]).standard_normal(out[name].shape)
        drawn = base * np.exp(spread * noise) if base else spread * noise
        out[name] = __import__('jax').numpy.asarray(drawn.astype(out[name].dtype))
    for name, factor in factors.items():
        out[name] = (out[name] * factor).astype(out[name].dtype)
    return out
```

```python
import numpy as np
import concourse.bass as bass
from concourse import mybir
from contextlib import ExitStack

D = 1024
SEQ = 256
STREAMS = 8
FRAMES = 16
T = 3
NTOK = T * 128
KD = D // 128
S5W = 512
NST = 16
HEADS = 4
DK = 128
DV = 256
GROUPS = 4
EXPERTS = 8
NEXP = GROUPS * EXPERTS
FF = 256
EPS = 1e-6
NCOND = 1 + STREAMS
CHUNK = 64
PAST = 256

CAP = 64
PAIRS = NEXP // 2
MAXPASS = NTOK // CAP
META = 4
NO_ROW = 4096

V_DT, V_ARE, V_AIM, V_N1, V_N2, V_D, V_BG, V_BR = 0, 16, 32, 48, 56, 64, 68, 72
V_N = 73
C_ID, C_UP, C_ONE, C_EB, C_EI, C_PT, C_HALF = 0, 128, 256, 384, 416, 448, 453
C_N = 456
R_ROPE, R_XI, R_KD, R_ZM = 0, 768, 832, 840
R_N = 872


def shape_constants():
    f = np.float32
    p = np.arange(128)
    c = np.zeros((128, C_N), f)
    c[:, C_ID:C_ID + 128] = np.eye(128)
    c[:, C_UP:C_UP + 128] = p[:, None] < p[None, :]
    c[:, C_ONE:C_ONE + 128] = 1.0
    e = np.arange(NEXP)
    c[:, C_EB:C_EB + 32] = PAIRS * CAP * (e % 2) + e // 2
    c[:, C_EI:C_EI + 32] = e
    c[:, C_PT:C_PT + 5] = CAP * np.arange(1, MAXPASS)
    c[:, C_HALF:C_HALF + 3] = -0.5
    stream = [np.zeros(128, int), np.zeros(128, int), p // FRAMES + 1]
    spread = np.zeros((128, 4, 2, 128), f)
    for j in range(4):
        for v, s in ((0, stream[0]), (1, stream[2])):
            spread[32 * j + s, j, v, p] = 1.0
    pos = np.stack([p, p + 128, PAST + p % FRAMES], 1).astype(f)
    theta = (1.0 / (10000.0 ** np.linspace(0.0, 1.0, DK // 2, dtype=f))).astype(f)
    ang = (pos[:, :, None] * theta).astype(f)
    r = np.zeros((128, R_N), f)
    s = f(DK ** -0.5)
    rope = np.stack([np.cos(ang), np.sin(ang), np.cos(ang) * s, np.sin(ang) * s], 2)
    r[:, R_ROPE:R_ROPE + 768] = rope.reshape(128, -1)
    lg = np.log(1.0 - 2.0 ** (-5.0 - np.arange(HEADS)))
    r[:, R_XI:R_XI + 64] = np.exp(lg[:, None] * (np.arange(FRAMES) + 1)).reshape(-1)
    r[:, R_KD:R_KD + 8] = np.exp(lg[None, None] * (SEQ - 1.0 - np.stack([p, p + 128], 1)[:, :, None])).reshape(128, 8)
    own = (p // FRAMES)[:, None, None] == np.arange(STREAMS)[None, None]
    r[:, R_ZM:R_ZM + 32] = (own * np.exp(lg[None, :, None] * (FRAMES - 1.0 - p % FRAMES)[:, None, None])).reshape(128, 32)
    n = np.arange(SEQ)
    full = np.exp(lg[:, None, None] * np.abs(n[:, None] - n[None, :])) * (n[:, None] // CHUNK <= n[None, :] // CHUNK)
    same = np.exp(lg[:, None, None] * np.abs(p[:, None] - p[None, :])) * (p[:, None] // FRAMES == p[None, :] // FRAMES)
    mask = np.concatenate([full[:, 0:128, :], full[:, 128:256, 128:256], same], 2).astype(f)
    starts = np.ones((128, NTOK), f)
    starts[:, SEQ::FRAMES] = 0.0
    rec = np.zeros((128, T, 2, META), np.int32)
    for k in range(2):
        rec[:, :, k, 0] = p[:, None] + 128 * np.arange(T)
        rec[:, :, k, 1] = rec[:, :, k, 0] + NTOK * k
    empty = np.zeros((MAXPASS * 128, PAIRS, META), np.int32)
    empty[:, :, 0:2] = NO_ROW
    return {"c_keep": c, "c_spread": spread.reshape(128, -1), "c_ret": r, "c_mask": mask, "c_starts": starts,
            "c_rec": rec.reshape(128, -1), "c_empty": empty.reshape(-1, META)}


def build(nc, A):
    f32, i32, f32r = mybir.dt.float32, mybir.dt.int32, mybir.dt.float32r
    ALU, ACT, AX = mybir.AluOpType, mybir.ActivationFunctionType, mybir.AxisListType
    MUL, ADD, SUB = ALU.mult, ALU.add, ALU.subtract
    ctx = ExitStack()
    with ctx:
        def sem(name):
            return ctx.enter_context(nc.semaphore(name))

        WORDS = 53200
        WEIGHTS = 24576
        base = (nc.sbuf_base + 31) // 32 * 32
        mem = [ctx.enter_context(nc.sbuf_tensor("weights", [128, WEIGHTS], f32)),
               ctx.enter_context(nc.sbuf_tensor("working", [128, WORDS - WEIGHTS], f32))]

        def shaped(v, *shape):
            if len(shape) == 1:
                return v
            names = " ".join(f"d{i}" for i in range(len(shape)))
            return v.rearrange(f"p ({names}) -> p {names}", **{f"d{i}": s for i, s in enumerate(shape)})

        def at(off, *shape, dt=None):
            n = int(np.prod(shape))
            assert off + n <= WEIGHTS or WEIGHTS <= off and off + n <= WORDS, (off, shape)
            v = mem[0][:, off:off + n] if off < WEIGHTS else mem[1][:, off - WEIGHTS:off - WEIGHTS + n]
            if dt is not None:
                v = v.bitcast(dt)
            return shaped(v, *shape)

        def part_at(off, *shape):
            n = int(np.prod(shape))
            if (off, n) not in part_tensors:
                part_tensors[off, n] = nc.alloc_sbuf_tensor_at(f"parts{off}", [128, n], f32r, offset=base + 4 * off)
            return shaped(part_tensors[off, n][:, :], *shape)

        part_tensors = {}

        class Region:

            def __init__(self, start, end):
                self.next, self.end = start, end

            def __call__(self, *shape, dt=None):
                o = self.next
                self.next += int(np.prod(shape))
                assert self.next <= self.end, (self.next, self.end)
                return at(o, *shape, dt=dt)

        PANEL, EXPERT, RING = 4096, 6144, 5
        SLOTS = 4 * EXPERT
        assert SLOTS == WEIGHTS
        UP, DOWN = KD * 2 * FF, 2 * D
        keep = Region(SLOTS, WORDS)
        const = keep(C_N)
        vecs = keep(76)
        condT = keep(KD, 32)
        modrow = keep(3, 512)
        scsh = keep(4, KD, NCOND)
        adab = keep(512)
        stat = keep(64)
        rec = keep(T, 2, META, dt=i32)
        recf = at(keep.next - T * 2 * META, T, 2, META)
        wr = keep(KD, 36)
        B0 = (keep.next + 7) // 8 * 8
        W0 = B0 + 12288
        nT = at(B0, KD, NTOK)
        qk = at(B0 + 3072, 2, T, 512)
        vv = at(B0 + 6144, T, 1024)
        gg = at(B0 + 9216, T, 1024)
        gates = at(B0 + 3072, T, 2048)
        x_in = at(B0 + 6144, T, D)
        bbraw = at(B0 + 9216, 2, NST, 32)
        bbar = at(B0 + 10240, 2, NST, 32)
        btmp = at(B0 + 11264, 2, NST, 32)
        sqj = at(B0 + 11264, 1024)
        early = Region(RING * PANEL, SLOTS)
        zT = early(4, NTOK)
        pw = early(2, NST, 40)
        ptmp = early(2, NST, 8)
        starts = early(NTOK)
        hfin = early(2, NST, NCOND)
        rc = at(WORDS - R_N, R_N)
        work = Region(W0, WORDS - R_N)
        uT = work(4, NTOK)
        rot = work(2, 2, 2, NTOK)
        rtmp = work(2, NTOK)
        m4 = work(4, NTOK)
        condraw = at(work.next - 4 * NTOK, KD, 32)
        hri = work(2, 2, NTOK)
        decay = work(NTOK)
        btp = work(2, 4, 128)
        ct = work(2, NST, 32)
        h0 = work(2, NST, STREAMS)
        disc = work(24, NST)
        oT = uT
        W1 = W0 + 1536
        ret = Region(W1, WORDS - R_N)
        qT = ret(HEADS, NTOK)
        kT = ret(HEADS, NTOK)
        rtm = at(ret.next, 4, T, HEADS, 64)
        qx = ret(HEADS, STREAMS, 32)
        sT = ret(2, 512)
        kz = ret(STREAMS, 128)
        kd = ret(2, 128)
        msk = ret(2, 512)
        s0a = ret(2, 4, DV)
        s0 = [s0a[:, 0], s0a[:, 1], at(RING * PANEL + 3072, 4, DV)]
        kvo = ret(DV)
        oj = ret(DV)
        highT = part_at(RING * PANEL, KD, NTOK)
        nTlow, oTlow, ogTlow = part_at(B0, KD, NTOK), part_at(W0, 4, NTOK), part_at(W1, KD, NTOK)
        out = Region(W1, WORDS)
        ogT = out(KD, NTOK)
        x2 = out(T, D)
        gte = out(2, D)
        spread = out(4, 2, 128)
        oThigh = part_at(out.next, 4, NTOK)
        fnorm = at(W1, D)
        route = Region(B0 + 3072, B0 + 6144)
        rtT = route(NTOK)
        lg = route(T, 36)
        e_in = route(15)
        e_out = route(15)
        goh = route(T, GROUPS)
        eoh = route(2, T, EXPERTS)
        el = route(T, EXPERTS)
        el2 = route(T, EXPERTS)
        tg = route(T, NEXP)
        tw = route(T, EXPERTS)
        t1 = route(T, 1)
        tm = route(2, T)
        foh = route(2, T, NEXP)
        sel = route(T, NEXP)
        rk = route(2, T)
        ps5 = route(2, T, 5)
        npass = route(2, T)
        brow = route(2, T)
        rowf = route(2, T)
        rowi = route(2, T, dt=i32)
        npcol = route(4)
        npi = route(4, dt=i32)
        gw = route(T)
        wk = route(2, T)
        metao = route.next
        metai = route(MAXPASS * PAIRS, META, dt=i32)
        metaf = at(metao, MAXPASS * PAIRS, META)
        gidx = route(2, 1, dt=i32)
        sidx = route(2, 1, dt=i32)
        gatecol = route(2, 1)
        moe = Region(B0 + 6144, B0 + 9216)
        xg = moe(2, D)
        hs = moe(2, FF)
        hT = moe(2, 2, 128)
        xgT = at(B0, 2, KD, 128)
        yb = at(B0 + 9216, 2, D)
        sq2 = at(W1, D)
        ys = at(0, T, 2, D)
        yout = at(6144, T, D)
        sq3 = at(9216, D)

        wup = at(0, 2, 2, UP)
        wdown = at(4 * UP, 2, 2, DOWN)

        ps = [ctx.enter_context(nc.psum_tensor(f"bank{i}", [128, 512], f32)) for i in range(8)]

        n2_d = nc.dram_tensor("n2_rows", (NTOK, D), f32).ap()
        meta_d = nc.dram_tensor("slot_records", (MAXPASS * 128 * PAIRS, META), i32).ap()
        y_d = nc.dram_tensor("expert_rows", (2 * NTOK, D), f32).ap()

        full = [sem(f"bank{i}_full") for i in range(8)]
        free = [sem(f"bank{i}_free") for i in range(8)]
        act_own, dve_own, pool_own = sem("act_own"), sem("dve_own"), sem("pool_own")
        panel_in = [sem(f"panel_in{i}") for i in range(RING)]
        names = ("const_in cond_in vecs_in x_in starts_in bb_in ct_in h0_in adab_in adab_later_in wr_in rec_in ret_in mask_in0 mask_in1 "
                 "s0_in0 s0_in1 s0_in2 spread_in x2_in fn_in meta_in ys_in0 ys_in1 ys_in2 "
                 "silu_c x_ssq x_ms x_rstd xn_ready scales1 scales3 prompt_xT prompt_x2T disc_exp expin_ready ang_ready disc_sin rotation_ready zeros_ready "
                 "bbar_ready bt_copied decay_ready rot_ready h_ready y_read h_copied z_ready oT_ready rope_done "
                 "qx_zero qx_ready kd_ready kz_ready o_ssq o_ms o_rstd og_ready merged x2_ready "
                 "n2_ssq n2_ms n2_rstd xn2_ready scsh2_ready e_in_ready e_out_ready sel_ready rows_ready rec_ready np_col "
                 "np_ready xg_zero w_split nT_split oT_split ogT_split mT_split up_in0 up_in1 down_in0 down_in1 gathered0 gathered1 scattered0 scattered1 tr_done "
                 "xgT_ready h_done silu_ready hs_ready hTp_done hT_ready y_done y_copied gate_copied gidx_copied sidx_copied x3_ready y3_ssq y3_ms "
                 "y3_rstd yout_ready hf_out kv_out s0_out0 s0_out1 s0_out2 n2_out empty_out recs_out y_out").split()
        S = {n: sem(n) for n in names}
        tally = {}

        class Own:

            def __init__(self, eng, own):
                self.eng, self.own = eng, own

            def __call__(self, ins, ready=None, frees=None):
                if frees is not None:
                    b, n = turns[frees]
                    ins.then_inc(free[b], 1)
                    self.eng.wait_ge(free[b], n)
                    return
                s = S[ready] if ready else self.own
                key = ready or id(s)
                tally[key] = tally.get(key, 0) + 1
                ins.then_inc(s, 1)
                self.eng.wait_ge(s, tally[key])

        turns = {}
        uses = [0] * 8
        rotating = [0]

        def turn(name, bank=None):
            if bank is None:
                bank = (0, 1, 2, 3, 7)[rotating[0] % 5]
                rotating[0] += 1
            if uses[bank]:
                nc.tensor.wait_ge(free[bank], uses[bank])
            uses[bank] += 1
            turns[name] = (bank, uses[bank])
            return ps[bank]

        def filled(ins, name):
            ins.then_inc(full[turns[name][0]], 1)

        def multiplied(eng, name):
            b, n = turns[name]
            eng.wait_ge(full[b], n)
            return ps[b]

        def copied(eng, name):
            b, n = turns[name]
            eng.wait_ge(free[b], n)

        panels = ([("ada", 0, j) for j in range(4)] + [("in", p) for p in range(7)] + [("glu", 0)]
                  + [("ada", m, j) for m in (1, 2) for j in range(4)] + [("in", p) for p in range(7, 11)]
                  + [("s5", 0)] + [("ret", h) for h in range(2)] + [("out", h) for h in range(2)])
        panel_at = {p: i for i, p in enumerate(panels)}
        LATE = panels.index(("in", 7))
        late = panels[LATE:]
        place = [i % RING if i < LATE else (i - LATE) % 3 for i in range(len(panels))]
        arrival = [place[:i].count(place[i]) + 1 for i in range(len(panels))]
        last_turn = {}
        src = {"ada": A["p_ada"], "in": A["p_in"], "glu": A["p_glu"], "s5": A["p_s5"], "ret": A["p_ret"], "out": A["p_out"]}

        def panel(key, kt, width):
            return at(place[panel_at[key]] * PANEL, kt, width)

        def panel_high(key, kt, width):
            return part_at((3 + late.index(key) % 2) * PANEL, kt, width)

        def panel_low(key, kt, width):
            return part_at(place[panel_at[key]] * PANEL, kt, width)

        def panel_arrived(eng, key):
            i = panel_at[key]
            eng.wait_ge(panel_in[place[i]], 16 * arrival[i])

        def last_users(i, words=None):
            lo, hi = words or (place[i] * PANEL, (place[i] + 1) * PANEL)
            found = {}
            for j in range(i):
                own = [place[j]] + ([3 + (j - LATE) % 2] if j >= LATE else [])
                for q in own:
                    if q * PANEL < hi and (q + 1) * PANEL > lo:
                        found[q] = j
            return sorted(set(found.values()))

        block = ctx.enter_context(nc.Block())
        ident = const[:, C_ID:C_ID + 128]

        @block.tensor
        def _(pe):
            mm = nc.tensor.matmul

            def transposes(name, pieces, bank=None):
                o = turn(name, bank)
                for off, n, m, piece in pieces:
                    ins = nc.tensor.transpose(o[0:n, off:off + m], piece, ident[0:m, 0:m])
                filled(ins, name)

            def ada(m):
                o = turn(("ada", m))
                for k in range(KD):
                    key = ("ada", m, k // 2)
                    if k % 2 == 0:
                        panel_arrived(pe, key)
                        last_turn[key] = ("ada", m)
                    for j in range(4):
                        ins = mm(o[32 * j:32 * j + 32, :], condT[:, k, :],
                                 panel(key, 2, 2048)[:, k % 2, 512 * j:512 * j + 512], start=k == 0, stop=k == KD - 1)
                filled(ins, ("ada", m))

            def adaT(m):
                copied(pe, ("ada", m))
                transposes(("adaT", m), [(128 * c, 128, 128, modrow[:, m, 128 * c:128 * c + 128]) for c in range(4)])

            def tok_gemm(name, key, t, lhs, kt, width=512, lo=0):
                wv = panel(key, kt, width)
                o = turn(name)
                for k in range(kt):
                    ins = mm(o[:, :], lhs[:, k, 128 * t:128 * t + 128], wv[:, k, lo:lo + 512], start=k == 0, stop=k == kt - 1)
                filled(ins, name)
                last_turn[key] = name

            def split_gemm(name, key, t, high, low, kt, width=512, lo=0, ready=None):
                whi, wlo = panel_high(key, kt, width), panel_low(key, kt, width)
                pe.wait_ge(S["w_split"], late.index(key) + 1)
                o = turn(name)
                for k in range(kt):
                    if ready and k % 2 == 0:
                        pe.wait_ge(S[ready], k // 2 + 1)
                    for n, (x, w) in enumerate(((high, whi), (high, wlo), (low, whi))):
                        ins = mm(o[:, :], x[:, k, 128 * t:128 * t + 128], w[:, k, lo:lo + 512],
                                 start=k == 0 and n == 0, stop=k == kt - 1 and n == 2)
                filled(ins, name)
                last_turn[key] = name

            def chan_gemm(name, key, c, rhs, kt, of=None):
                wv = panel(key, kt, 512)
                o = turn(name)
                for k in range(kt):
                    if of:
                        copied(pe, (of, k))
                    ins = mm(o[:, 0:NTOK], wv[:, k, 128 * c:128 * c + 128], rhs[:, k, :], start=k == 0, stop=k == kt - 1)
                filled(ins, name)
                last_turn[key] = name

            def x_transposes(k, bank=None):
                transposes(("xT", k), [(128 * t, 128, 128, x_in[:, t, 128 * k:128 * k + 128]) for t in range(T)], bank)

            pe.wait_ge(S["const_in"], 16)
            pe.wait_ge(S["xn_ready"], T)
            for k in range(3):
                x_transposes(k, 4 + k)
            for k in range(3, 6):
                x_transposes(k)
            pe.wait_ge(S["silu_c"], 1)
            ada(0)
            adaT(0)
            for k in range(6, KD):
                x_transposes(k)
            panel_arrived(pe, ("in", 0))
            for c in range(4):
                chan_gemm(("u", c), ("in", 0), c, nT, KD, "xT" if c == 0 else None)

            def b_transposes(a):
                if a == 0:
                    pe.wait_ge(S["bbar_ready"], 2)
                transposes(("BT", a), [(128 * r, 128, 128, at(B0 + 10240 + 512 * r + 128 * a, 128)) for r in range(2)])

            def bu(i):
                a, q = divmod(i, 4)
                if q == 0:
                    copied(pe, ("u", a))
                    pe.wait_ge(S["bt_copied"], 8 * (a + 1))
                for r in range(2):
                    o = turn(("bu", i, r), 5 + r)
                    filled(mm(o[:, 0:NTOK], btp[:, r, q, :], uT[:, a, :], start=True, stop=True), ("bu", i, r))

            def y_sum(i):
                a, q = divmod(i, 4)
                pe.wait_ge(S["h_ready"], 2 * (i + 1))
                if q == 0:
                    turn(("y", a), 4)
                if i == 0:
                    pe.wait_ge(S["ct_in"], 16)
                mm(ps[4][32 * q:32 * q + 32, 0:NTOK], ct[:, 0, i, :], hri[:, i % 2, 0, :], start=True, stop=False)
                ins = mm(ps[4][32 * q:32 * q + 32, 0:NTOK], ct[:, 1, i, :], hri[:, i % 2, 1, :], start=False, stop=True)
                ins.then_inc(S["y_read"], 1)

            b_transposes(0)
            for j in range(18):
                if j < NST:
                    bu(j)
                    if j % 4 == 3 and j < NST - 1:
                        b_transposes(j // 4 + 1)
                key = ("in", 1 + j // 3)
                if j % 3 == 0:
                    panel_arrived(pe, key)
                tok_gemm((*key, j % 3), key, j % 3, nT, KD)
                if j >= 2:
                    y_sum(j - 2)
            pe.wait_ge(S["z_ready"], 4)
            panel_arrived(pe, ("glu", 0))
            for c in range(4):
                chan_gemm(("glu", c), ("glu", 0), c, zT, 4)
            ada(1)
            pe.wait_ge(S["rope_done"], 4)
            for r, n in ((0, "qT"), (1, "kT")):
                for h in range(HEADS):
                    transposes((n, h), [(128 * t, 128, 128, qk[:, r, t, 128 * h:128 * h + 128]) for t in range(T)])

            def scores(h):
                copied(pe, ("qT", h))
                copied(pe, ("kT", h))
                o = turn(("s", h))
                mm(o[:, 0:256], kT[:, h, 0:128], qT[:, h, 0:256], start=True, stop=True)
                mm(o[:, 256:384], kT[:, h, 128:256], qT[:, h, 128:256], start=True, stop=True)
                filled(mm(o[:, 384:512], kT[:, h, 256:384], qT[:, h, 256:384], start=True, stop=True), ("s", h))

            def head(h):
                lo = DV * h
                pe.wait_ge(S["kd_ready"], 2 * (h + 1))
                o = turn(("kvp", h))
                mm(o[:, 0:DV], kd[:, 0, :], vv[:, 0, lo:lo + DV], start=True, stop=False)
                filled(mm(o[:, 0:DV], kd[:, 1, :], vv[:, 1, lo:lo + DV], start=False, stop=True), ("kvp", h))
                pe.wait_ge(S["kz_ready"], h + 1)
                for b2 in range(4):
                    o = turn(("kvs", h, b2))
                    for r in range(2):
                        ins = mm(o[:, DV * r:DV * r + DV], kz[:, 2 * b2 + r, :], vv[:, 2, lo:lo + DV], start=True, stop=True)
                    filled(ins, ("kvs", h, b2))
                if h + 1 < HEADS:
                    scores(h + 1)
                copied(pe, ("s", h))
                o = turn(("oA", h), 5)
                mm(o[:, 0:DV], sT[:, h % 2, 0:128], vv[:, 0, lo:lo + DV], start=True, stop=True)
                mm(o[:, DV:2 * DV], sT[:, h % 2, 128:256], vv[:, 0, lo:lo + DV], start=True, stop=False)
                filled(mm(o[:, DV:2 * DV], sT[:, h % 2, 256:384], vv[:, 1, lo:lo + DV], start=False, stop=True), ("oA", h))
                o = turn(("oB", h), 6)
                mm(o[:, 0:DV], sT[:, h % 2, 384:512], vv[:, 2, lo:lo + DV], start=True, stop=False, skip_group_check=True)
                pe.wait_ge(S["qx_ready"], 2 * HEADS)
                for half in range(2):
                    n = 2 * h + half
                    pe.wait_ge(S[f"s0_in{n % 3}"], 16 * (n // 3 + 1))
                    for b in range(4):
                        b8 = 4 * half + b
                        j = 32 * (b8 // 2)
                        ins = mm(o[j:j + 32, 0:DV], qx[:, h, b8, :], s0[n % 3][:, b, :], start=False, stop=b8 == 7,
                                 skip_group_check=True)
                filled(ins, ("oB", h))

            scores(0)
            head(0)
            adaT(1)
            head(1)
            ada(2)
            head(2)
            adaT(2)
            head(3)
            pe.wait_ge(S["nT_split"], 1)
            for p in range(7, 11):
                for t in range(T):
                    split_gemm(("in", p, t), ("in", p), t, highT, nTlow, KD)
            pe.wait_ge(S["og_ready"], T * HEADS)
            for k in range(KD):
                transposes(("ogT", k), [(128 * t, 128, 128, gg[:, t, 128 * k:128 * k + 128]) for t in range(T)])
            pe.wait_ge(S["oT_split"], 1)
            for hf in range(2):
                for t in range(T):
                    split_gemm(("ya", hf, t), ("s5", 0), t, oThigh, oTlow, 4, 1024, 512 * hf)
            for hf in range(2):
                for t in range(T):
                    split_gemm(("yb", hf, t), ("ret", hf), t, highT, ogTlow, KD, ready="ogT_split")

            def gate_rows(name, m):
                for v in range(2):
                    for hf in range(2):
                        o = turn((name, v, hf))
                        j = hf if m == 1 else 2 + hf
                        filled(mm(o[:, :], spread[:, j, v, :], modrow[:, m, :], start=True, stop=True), (name, v, hf))

            pe.wait_ge(S["spread_in"], 16)
            gate_rows("g1", 1)
            pe.wait_ge(S["merged"], 6)
            for k in range(KD):
                transposes(("mT", k), [(128 * t, 128, 128, gates[:, t, 128 * k:128 * k + 128]) for t in range(T)])
            for hf in range(2):
                for t in range(T):
                    split_gemm(("wo", hf, t), ("out", hf), t, highT, nTlow, KD, ready="mT_split")
            gate_rows("g2", 2)
            pe.wait_ge(S["xn2_ready"], T)
            for k in range(KD):
                transposes(("x2T", k), [(128 * t, 128, 128, gg[:, t, 128 * k:128 * k + 128]) for t in range(T)])
            for k in range(KD):
                copied(pe, ("x2T", k))
            pe.wait_ge(S["wr_in"], 16)
            o = turn("router")
            for k in range(KD):
                ins = mm(o[0:36, 0:NTOK], wr[:, k, :], nT[:, k, :], start=k == 0, stop=k == KD - 1)
            filled(ins, "router")
            for t in range(T):
                for hf in range(2):
                    transposes(("n2", t, hf), [(128 * c, 128, 128, nT[:, 4 * hf + c, 128 * t:128 * t + 128]) for c in range(4)])
                if t == 0:
                    copied(pe, "router")
                    transposes("logits", [(36 * s, 128, 36, rtT[0:36, 128 * s:128 * s + 128]) for s in range(T)])
            pe.wait_ge(S["sel_ready"], 1)
            o = turn("rank")
            for t in range(T):
                for s in range(t + 1):
                    lhs = const[:, C_UP:C_UP + 128] if s == t else const[:, C_ONE:C_ONE + 128]
                    ins = mm(o[:, NEXP * t:NEXP * t + NEXP], lhs, sel[:, s, :], start=s == 0, stop=s == t)
            filled(ins, "rank")
            pe.wait_ge(S["np_col"], 1)
            transposes("np", [(0, 1, 128, npcol[:, 0:1])])
            for b in range(8):
                if uses[b]:
                    pe.wait_ge(free[b], uses[b])
            pe.wait_ge(S["np_ready"], 1)
            passes = pe.value_load(npi[0:1, 0:1], min_val=1, max_val=MAXPASS)

            def rows_by_channel(t, u):
                i = 2 * t + u
                pe.wait_ge(S[f"gathered{u}"], 16 * t + 16)
                if not (isinstance(i, int) and i == 0):
                    pe.wait_ge(S["xgT_ready"], 2 * i)
                for k in range(KD):
                    ins = nc.tensor.transpose(ps[k // 4][:, 128 * (k % 4):128 * (k % 4) + 128],
                                              xg[:, u, 128 * k:128 * k + 128], ident)
                ins.then_inc(S["tr_done"], 1)

            def up(t, u, first=False):
                i = 2 * t + u
                pe.wait_ge(S[f"up_in{u}"], 16 * t + 16)
                pe.wait_ge(S["xgT_ready"], 2 * i + 2)
                if not first:
                    pe.wait_ge(S["hs_ready"], i - 1)
                for k in range(KD):
                    for e in range(2):
                        ins = mm(ps[2 + u][64 * e:64 * e + 64, :], xgT[:, u, k, 64 * e:64 * e + 64],
                                 wup[:, u, e, 512 * k:512 * k + 512], start=k == 0, stop=k == KD - 1)
                ins.then_inc(S["h_done"], 1)

            def hidden_by_channel(t, u):
                i = 2 * t + u
                pe.wait_ge(S["hs_ready"], i + 1)
                if not (isinstance(i, int) and i == 0):
                    pe.wait_ge(S["hT_ready"], i)
                for k in range(2):
                    ins = nc.tensor.transpose(ps[4][:, 128 * k:128 * k + 128], hs[:, u, 128 * k:128 * k + 128], ident)
                ins.then_inc(S["hTp_done"], 1)

            def down(t, u):
                i = 2 * t + u
                pe.wait_ge(S[f"down_in{u}"], 16 * t + 16)
                pe.wait_ge(S["hT_ready"], i + 1)
                if not (isinstance(i, int) and i == 0):
                    pe.wait_ge(S["y_copied"], 2 * i)
                for hf in range(2):
                    for k in range(2):
                        for e in range(2):
                            o_ = 1024 * k + 512 * hf
                            ins = mm(ps[5 + hf][64 * e:64 * e + 64, :], hT[:, u, k, 64 * e:64 * e + 64],
                                     wdown[:, u, e, o_:o_ + 512], start=k == 0, stop=k == 1)
                ins.then_inc(S["y_done"], 1)

            LAST = PAIRS // 2 - 1
            rows_by_channel(0, 0)
            up(0, 0, True)
            rows_by_channel(0, 1)
            hidden_by_channel(0, 0)
            up(0, 1, True)
            with pe.Fori(1, PAIRS // 2) as t:
                rows_by_channel(t, 0)
                down(t - 1, 0)
                hidden_by_channel(t - 1, 1)
                up(t, 0)
                rows_by_channel(t, 1)
                down(t - 1, 1)
                hidden_by_channel(t, 0)
                up(t, 1)
            down(LAST, 0)
            hidden_by_channel(LAST, 1)
            down(LAST, 1)
            with pe.If(passes > 1):
                with pe.Fori(PAIRS // 2, passes * (PAIRS // 2)) as t:
                    for u in range(2):
                        rows_by_channel(t, u)
                        up(t, u)
                        hidden_by_channel(t, u)
                        down(t, u)

        @block.sync
        def _(sp):
            for t in range(T):
                sp.dma_start(x_in[:, t, :], A["x"][t, :, :]).then_inc(S["x_in"], 16)
            for i, key in enumerate(panels):
                if key == ("ada", 2, 2):
                    sp.wait_ge(S["s0_in0"], 16 * 2)
                if key == ("in", 8):
                    sp.wait_ge(S["s0_in1"], 16 * 3)
                for j in last_users(i):
                    multiplied(sp, last_turn[panels[j]])
                n = 2048 if key[0] == "glu" else PANEL
                d = src[key[0]][4 * key[1] + key[2] if key[0] == "ada" else key[1], :, :]
                sp.dma_start(at(place[i] * PANEL, n), d).then_inc(panel_in[place[i]], 16)

            def free_place(lo, hi):
                for j in last_users(len(panels), (lo, hi)):
                    multiplied(sp, last_turn[panels[j]])

            for u in range(2):
                free_place(u * 2 * UP, (u + 1) * 2 * UP)
                sp.dma_start(wup[:, u], A["p_up"][u, :, :, :]).then_inc(S[f"up_in{u}"], 16)
                if u == 0:
                    sp.wait_ge(S["hf_out"], 16)
                free_place(4 * UP + u * 2 * DOWN, 4 * UP + (u + 1) * 2 * DOWN)
                sp.dma_start(wdown[:, u], A["p_down"][u, :, :, :]).then_inc(S[f"down_in{u}"], 16)

            def load(t, m, u):
                sp.wait_ge(S["h_done"], 2 * t + u - 1)
                sp.dma_start(wup[:, u], A["p_up"][2 * m + u, :, :, :]).then_inc(S[f"up_in{u}"], 16)
                sp.wait_ge(S["y_done"], 2 * t + u - 1)
                sp.dma_start(wdown[:, u], A["p_down"][2 * m + u, :, :, :]).then_inc(S[f"down_in{u}"], 16)

            with sp.Fori(1, PAIRS // 2) as t:
                load(t, t, 0)
                load(t, t, 1)
            sp.wait_ge(S["np_ready"], 1)
            passes = sp.value_load(npi[0:1, 0:1], min_val=1, max_val=MAXPASS)
            with sp.If(passes > 1):
                with sp.Fori(PAIRS // 2, passes * (PAIRS // 2)) as t:
                    load(t, t % (PAIRS // 2), 0)
                    load(t, t % (PAIRS // 2), 1)

        @block.scalar
        def _(act):
            run = Own(act, act_own)
            A_ = nc.scalar.activation
            cp = nc.scalar.copy
            act.dma_start(vecs[:, 0:V_N], A["vecs"]).then_inc(S["vecs_in"], 16)
            act.dma_start(condraw, A["condT"]).then_inc(S["cond_in"], 16)
            act.dma_start(const, A["c_keep"]).then_inc(S["const_in"], 16)
            act.dma_start(adab, A["b_ada"][0, :, :]).then_inc(S["adab_in"], 16)
            act.wait_ge(S["cond_in"], 16)
            run(A_(condT, condraw, ACT.Silu), "silu_c")
            act.wait_ge(S["x_in"], 16 * T)
            for t in range(T):
                run(A_(sqj, x_in[:, t, :], ACT.Square, accum_out=stat[:, t:t + 1]), "x_ssq")
            act.dma_start(bbraw, A["bb"]).then_inc(S["bb_in"], 16)
            act.dma_start(starts, A["c_starts"]).then_inc(S["starts_in"], 16)
            act.dma_start(h0, A["h0"]).then_inc(S["h0_in"], 16)
            act.dma_start(ct, A["ct"]).then_inc(S["ct_in"], 16)
            act.dma_start(wr, A["w_router"]).then_inc(S["wr_in"], 16)
            act.dma_start(rec, A["c_rec"]).then_inc(S["rec_in"], 16)
            act.dma_start(rc, A["c_ret"]).then_inc(S["ret_in"], 16)
            act.wait_ge(S["vecs_in"], 16)
            run(A_(disc[:, 0, :], vecs[:, V_DT:V_DT + NST], ACT.Exp), "disc_exp")
            act.wait_ge(S["expin_ready"], 1)
            run(A_(disc[:, 2, :], disc[:, 1, :], ACT.Exp), "disc_exp")
            act.wait_ge(S["ang_ready"], 1)
            run(A_(disc[:, 5, :], disc[:, 4, :], ACT.Sin), "disc_sin")
            run(A_(disc[:, 6, :], disc[:, 4, :], ACT.Sin, scale=0.5), "disc_sin")

            def mod_columns(m):
                o = multiplied(act, ("adaT", m)).rearrange("p (c j s) -> p c j s", c=4, j=4)
                pieces = [(h, v, j) for h, v in {0: [(0, 0), (1, 1)], 1: [(1, 2)], 2: [(0, 3)]}[m] for j in range(2)]
                for n, (half, vec, j) in enumerate(pieces):
                    run(cp(scsh[:, vec, 4 * j:4 * j + 4, :], o[:, :, 2 * half + j, 0:NCOND]),
                        frees=("adaT", m) if n == len(pieces) - 1 else None)

            def modulate(name, sc, sh):
                act.wait_ge(S[f"scales{sc}"], 1)
                for k in range(KD):
                    o = multiplied(act, (name, k))
                    run(A_(nT[:, k, 0:SEQ], o[:, 0:SEQ], ACT.Identity, scale=scsh[:, sc, k, 0:1], bias=scsh[:, sh, k, 0:1]),
                        f"prompt_{name}")

            mod_columns(0)
            modulate("xT", 1, 0)
            for c in range(4):
                o = multiplied(act, ("u", c))
                run(cp(uT[:, c, :], o[:, 0:NTOK]), frees=("u", c))

            def bt_copy(a):
                if a == 0:
                    act.wait_ge(S["zeros_ready"], 1)
                else:
                    multiplied(act, ("bu", 4 * a - 1, 1))
                o = multiplied(act, ("BT", a))
                for r in range(2):
                    for q in range(4):
                        run(cp(btp[32 * q:32 * q + 32, r, q, :], o[32 * q:32 * q + 32, 128 * r:128 * r + 128]), "bt_copied")
                run(cp(stat[:, 60:61], o[:, 0:1]), frees=("BT", a))

            def decays(i):
                if i == 0:
                    act.wait_ge(S["starts_in"], 16)
                else:
                    act.wait_ge(S["h_ready"], 2 * i)
                run(A_(decay, starts, ACT.Copy, scale=disc[:, 2, i:i + 1]), "decay_ready")

            def last_states(i):
                act.wait_ge(S["h_ready"], 2 * i + 2)
                for r in range(2):
                    run(cp(hfin[:, r, i, :], hri[:, i % 2, r, SEQ - 1::FRAMES]), "h_copied")

            bt_copy(0)
            for j in range(18):
                if j < NST:
                    decays(j)
                p, t = 1 + j // 3, j % 3
                o = multiplied(act, ("in", p, t))
                if p <= 2:
                    run(cp(qk[:, p - 1, t, :], o[:, :]), frees=("in", p, t))
                elif p <= 4:
                    run(cp(vv[:, t, 512 * (p - 3):512 * (p - 3) + 512], o[:, :]), frees=("in", p, t))
                else:
                    run(A_(gg[:, t, 512 * (p - 5):512 * (p - 5) + 512], o[:, :], ACT.Silu), frees=("in", p, t))
                if j % 4 == 3 and j < NST - 1:
                    bt_copy(j // 4 + 1)
                if j < NST:
                    last_states(j)
            act.dma_start(A["o_s5"], hfin).then_inc(S["hf_out"], 16)
            for a in range(4):
                copied(act, ("y", a))
                run(A_(zT[:, a, :], zT[:, a, :], ACT.Gelu_apprx_tanh), "z_ready")
            for c in range(4):
                o = multiplied(act, ("glu", c))
                run(A_(uT[:, c, :], o[:, 0:NTOK], ACT.Sigmoid, bias=vecs[:, V_BG + c:V_BG + c + 1]), frees=("glu", c))
            for n, dst in (("qT", qT), ("kT", kT)):
                for h in range(HEADS):
                    o = multiplied(act, (n, h))
                    run(cp(dst[:, h, :], o[:, 0:NTOK]), frees=(n, h))

            def o_squares(h):
                for t in range(T):
                    o = multiplied(act, ("oA", h) if t < 2 else ("oB", h))
                    run(A_(oj, o[:, DV * (t % 2):DV * (t % 2) + DV], ACT.Square,
                           accum_out=stat[:, 8 + T * h + t:9 + T * h + t]), "o_ssq")

            o_squares(0)
            mod_columns(1)
            o_squares(1)
            o_squares(2)
            mod_columns(2)
            o_squares(3)
            act.wait_ge(S["og_ready"], T * HEADS)
            for p in range(7, 11):
                for t in range(T):
                    o = multiplied(act, ("in", p, t))
                    run(A_(gates[:, t, 512 * (p - 7):512 * (p - 7) + 512], o[:, :], ACT.Sigmoid), frees=("in", p, t))
            for k in range(KD):
                o = multiplied(act, ("ogT", k))
                run(cp(ogT[:, k, :], o[:, 0:NTOK]), frees=("ogT", k))
            for r, n in enumerate((3, 3, 2)):
                act.wait_ge(S[f"s0_out{r}"], 16 * n)
            act.wait_ge(S["kv_out"], 16 * HEADS)
            for v in range(2):
                for hf in range(2):
                    o = multiplied(act, ("g1", v, hf))
                    run(cp(gte[:, v, 512 * hf:512 * hf + 512], o[:, :]), frees=("g1", v, hf))
            for k in range(KD):
                o = multiplied(act, ("mT", k))
                run(cp(nT[:, k, :], o[:, 0:NTOK]), frees=("mT", k))
            act.wait_ge(S["x2_ready"], 6)
            for t in range(T):
                run(A_(sq2, x2[:, t, :], ACT.Square, accum_out=stat[:, 24 + t:25 + t]), "n2_ssq")
            for v in range(2):
                for hf in range(2):
                    o = multiplied(act, ("g2", v, hf))
                    run(cp(gte[:, v, 512 * hf:512 * hf + 512], o[:, :]), frees=("g2", v, hf))
            modulate("x2T", 3, 2)
            o = multiplied(act, "router")
            run(A_(rtT[0:36, :], o[0:36, 0:NTOK], ACT.Identity, bias=vecs[0:36, V_BR:V_BR + 1]), frees="router")
            for t in range(T):
                for hf in range(2):
                    o = multiplied(act, ("n2", t, hf))
                    run(cp(gg[:, t, 512 * hf:512 * hf + 512], o[:, :]), frees=("n2", t, hf))
                act.dma_start(n2_d[128 * t:128 * t + 128, :], gg[:, t, :]).then_inc(S["n2_out"], 16)
            act.wait_ge(S["e_in_ready"], 2)
            run(A_(e_out, e_in, ACT.Exp), "e_out_ready")
            act.wait_ge(S["n2_out"], 16 * T)
            act.wait_ge(S["np_ready"], 1)
            passes = act.value_load(npi[0:1, 0:1], min_val=1, max_val=MAXPASS)

            def rows_copy(t, u, first=False):
                i = 2 * t + u
                act.wait_ge(S["tr_done"], i + 1)
                if not first:
                    act.wait_ge(S["h_done"], i - 1)
                for c in range(2):
                    cp(at(B0 + u * 1024 + 512 * c, 512), ps[c][:, :]).then_inc(S["xgT_ready"], 1)

            def silu(t, u, first=False):
                i = 2 * t + u
                act.wait_ge(S["h_done"], i + 1)
                if not first:
                    act.wait_ge(S["hTp_done"], i - 1)
                A_(hs[:, u, :], ps[2 + u][:, 0:FF], ACT.Silu).then_inc(S["silu_ready"], 1)
                if not first:
                    act.wait_ge(S["y_copied"], 2 * i - 2)
                cp(gatecol[:, u, :], metaf[:, bass.ds(i, 1), 2]).then_inc(S["gate_copied"], 1)

            def rows_out(t, u, first=False):
                i = 2 * t + u
                act.wait_ge(S["y_done"], i + 1)
                act.wait_ge(S["gate_copied"], i + 1)
                if not first:
                    act.wait_ge(S[f"scattered{u}"], 16 * t)
                for hf in range(2):
                    A_(yb[:, u, 512 * hf:512 * hf + 512], ps[5 + hf][:, :], ACT.Copy, scale=gatecol[:, u, :])\
                        .then_inc(S["y_copied"], 1)

            LAST = PAIRS // 2 - 1
            rows_copy(0, 0, True)
            silu(0, 0, True)
            rows_copy(0, 1, True)
            silu(0, 1, True)
            for t, first in ((1, True),):
                rows_copy(t, 0)
                rows_out(t - 1, 0, first)
                silu(t, 0)
                rows_copy(t, 1)
                rows_out(t - 1, 1, first)
                silu(t, 1)
            with act.Fori(2, PAIRS // 2) as t:
                rows_copy(t, 0)
                rows_out(t - 1, 0)
                silu(t, 0)
                rows_copy(t, 1)
                rows_out(t - 1, 1)
                silu(t, 1)
            rows_out(LAST, 0)
            rows_out(LAST, 1)
            with act.If(passes > 1):
                with act.Fori(PAIRS // 2, passes * (PAIRS // 2)) as t:
                    for u in range(2):
                        rows_copy(t, u)
                        silu(t, u)
                        rows_out(t, u)
            for t in range(T):
                act.wait_ge(S["x3_ready"], t + 1)
                run(A_(sq3, x2[:, t, :], ACT.Square, accum_out=stat[:, 40 + t:41 + t]), "y3_ssq")
            for t in range(T):
                act.wait_ge(S["yout_ready"], t + 1)
                act.dma_start(A["o_y"][t, :, :], yout[:, t, :]).then_inc(S["y_out"], 16)
            act.wait_ge(S["y_out"], 16 * T)
            act.wait_ge(S["hf_out"], 16)

        @block.vector
        def _(dve):
            run = Own(dve, dve_own)
            tt, ts, stt = nc.vector.tensor_tensor, nc.vector.tensor_scalar, nc.vector.scalar_tensor_tensor
            tred = nc.vector.tensor_reduce

            def bc(v, axis, n):
                v = v.unsqueeze(axis)
                shape = list(v.shape)
                shape[axis] = n
                return v.broadcast_to(shape)

            dve.wait_ge(S["x_ssq"], T)
            run(ts(stat[:, 4:7], stat[:, 0:3], 1.0 / D, EPS, MUL, ADD), "x_ms")
            are, aim = vecs[:, V_ARE:V_ARE + NST], vecs[:, V_AIM:V_AIM + NST]
            d_ = lambda n: disc[:, n, :]
            dve.wait_ge(S["disc_exp"], 1)
            run(tt(d_(1), are, d_(0), MUL), "expin_ready")
            run(tt(d_(3), aim, d_(0), MUL))
            MAGIC = 12582912.0
            run(ts(d_(7), d_(3), float(1 / (2 * np.pi)), MAGIC, MUL, ADD))
            run(ts(d_(7), d_(7), MAGIC, None, SUB))
            c1 = 6.28125
            c2 = float(np.float32(2 * np.pi - c1))
            c3 = float(2 * np.pi - c1 - c2)
            run(stt(d_(3), d_(7), -c1, d_(3), MUL, ADD))
            run(stt(d_(3), d_(7), -c2, d_(3), MUL, ADD))
            run(stt(d_(4), d_(7), -c3, d_(3), MUL, ADD))
            PI = 3.1415925
            run(ts(d_(4), d_(4), PI, -PI, ALU.min, ALU.max), "ang_ready")
            dve.wait_ge(S["x_rstd"], 1)
            for t in range(T):
                run(ts(x_in[:, t, :], x_in[:, t, :], stat[:, 48 + t:49 + t], None, MUL), "xn_ready")
            dve.wait_ge(S["disc_sin"], 2)
            run(tt(d_(7), d_(6), d_(6), MUL))
            run(ts(d_(6), d_(7), -2.0, 1.0, MUL, ADD), "rotation_ready")
            run(tt(d_(8), d_(2), d_(6), MUL))
            run(ts(d_(8), d_(8), 1.0, None, SUB))
            run(tt(d_(9), d_(2), d_(5), MUL))
            run(tt(d_(10), are, are, MUL))
            run(tt(d_(11), aim, aim, MUL))
            run(tt(d_(10), d_(10), d_(11), ADD))
            run(nc.vector.reciprocal(d_(10), d_(10)))
            run(tt(d_(11), d_(8), are, MUL))
            run(tt(d_(12), d_(9), aim, MUL))
            run(tt(d_(11), d_(11), d_(12), ADD))
            run(tt(d_(11), d_(11), d_(10), MUL))
            run(tt(d_(12), d_(9), are, MUL))
            run(tt(d_(13), d_(8), aim, MUL))
            run(tt(d_(12), d_(12), d_(13), SUB))
            run(tt(d_(12), d_(12), d_(10), MUL))
            def mod_rows(m):
                o = multiplied(dve, ("ada", m))
                if m == 0:
                    dve.wait_ge(S["adab_in"], 16)
                else:
                    dve.wait_ge(S["adab_later_in"], 16 * m)
                run(tt(modrow[:, m, :], o[:, :], adab, ADD), frees=("ada", m))

            def scales(vec, norm, m):
                copied(dve, ("adaT", m))
                run(stt(scsh[:, vec], scsh[:, vec], 1.0, bc(vecs[:, norm:norm + KD], 2, NCOND), ADD, MUL), f"scales{vec}")

            def modulate(name, sc, sh):
                for k in range(KD):
                    o = multiplied(dve, (name, k))
                    dve.wait_ge(S[f"prompt_{name}"], k + 1)
                    smp = nT[:, k, SEQ:NTOK].rearrange("p (b f) -> p b f", f=FRAMES)
                    run(tt(smp, o[:, SEQ:NTOK].rearrange("p (b f) -> p b f", f=FRAMES),
                           bc(scsh[:, sc, k, 1:NCOND], 2, FRAMES), MUL))
                    run(tt(smp, smp, bc(scsh[:, sh, k, 1:NCOND], 2, FRAMES), ADD), frees=(name, k))

            mod_rows(0)
            scales(1, V_N1, 0)
            modulate("xT", 1, 0)
            fre, fim = bc(d_(11), 2, 32), bc(d_(12), 2, 32)
            dve.wait_ge(S["bb_in"], 16)
            run(tt(btmp[:, 0], bbraw[:, 0], fre, MUL))
            run(tt(btmp[:, 1], bbraw[:, 1], fim, MUL))
            run(tt(bbar[:, 0], btmp[:, 0], btmp[:, 1], SUB), "bbar_ready")
            run(tt(btmp[:, 0], bbraw[:, 1], fre, MUL))
            run(tt(btmp[:, 1], bbraw[:, 0], fim, MUL))
            run(tt(bbar[:, 1], btmp[:, 0], btmp[:, 1], ADD), "bbar_ready")
            dve.wait_ge(S["h0_in"], 16)
            for r in range(2):
                run(tt(h0[:, r], h0[:, r], bc(d_(2), 2, STREAMS), MUL))
            dve.wait_ge(S["ct_in"], 16)
            run(ts(ct[:, 1], ct[:, 1], -1.0, None, MUL))


            def state_tile(i):
                tre, tim = rot[:, (i // 2) % 2, 0, i % 2, :], rot[:, (i // 2) % 2, 1, i % 2, :]
                m = [m4[:, n, :] for n in range(4)]
                dve.wait_ge(S["rot_ready"], 2 * (i // 2 + 1))
                o = multiplied(dve, ("bu", i, 0))[:, 0:NTOK]
                run(tt(m[0], tre, o, MUL))
                run(tt(m[1], tim, o, MUL), frees=("bu", i, 0))
                o = multiplied(dve, ("bu", i, 1))[:, 0:NTOK]
                run(tt(m[2], tre, o, MUL))
                run(tt(m[3], tim, o, MUL), frees=("bu", i, 1))
                run(tt(m[0], m[0], m[3], ADD))
                run(tt(m[2], m[2], m[1], SUB))
                for r in range(2):
                    run(tt(m[2 * r][:, SEQ::FRAMES], m[2 * r][:, SEQ::FRAMES], h0[:, r, i, :], ADD))
                dve.wait_ge(S["decay_ready"], i + 1)
                run(nc.vector.tensor_tensor_scan(m[1], decay, m[0], 0.0, MUL, ADD))
                run(nc.vector.tensor_tensor_scan(m[3], decay, m[2], 0.0, MUL, ADD))
                if i >= 2:
                    dve.wait_ge(S["y_read"], i - 1)
                    dve.wait_ge(S["h_copied"], 2 * (i - 1))
                run(tt(m[0], tre, m[1], MUL))
                run(tt(m[2], tim, m[3], MUL))
                run(tt(hri[:, i % 2, 0, :], m[0], m[2], SUB), "h_ready")
                run(tt(m[0], tim, m[1], MUL))
                run(tt(m[2], tre, m[3], MUL))
                run(tt(hri[:, i % 2, 1, :], m[0], m[2], ADD), "h_ready")

            def skip(a):
                o = ps[4]
                dve.wait_ge(S["y_read"], 4 * (a + 1))
                run(stt(zT[:, a, :], uT[:, a, :], vecs[:, V_D + a:V_D + a + 1], o[:, 0:NTOK], MUL, ADD), frees=("y", a))

            for i in range(NST):
                state_tile(i)
                if i % 4 == 1 and i > 4:
                    skip(i // 4 - 1)
            skip(3)
            dve.wait_ge(S["ret_in"], 16)
            rope = rc[:, R_ROPE:R_ROPE + 768].rearrange("p (t s d) -> p t s d", t=T, s=4)
            tmp = [rtm[:, n] for n in range(4)]
            for r in range(2):
                for t in range(T):
                    copied(dve, ("in", 1 + r, t))
                x1, x2_ = (qk[:, r].rearrange("p t (h s d) -> p t h s d", h=HEADS, s=2)[:, :, :, s, :] for s in range(2))
                cos, sin = (bc(rope[:, :, 2 * r + s, :], 2, HEADS) for s in range(2))
                run(tt(tmp[0], x1, cos, MUL))
                run(tt(tmp[1], x2_, sin, MUL))
                run(tt(tmp[2], x1, sin, MUL))
                run(tt(tmp[3], x2_, cos, MUL))
                run(tt(x1, tmp[0], tmp[1], SUB), "rope_done")
                run(tt(x2_, tmp[2], tmp[3], ADD), "rope_done")
            for c in range(4):
                copied(dve, ("glu", c))
                run(tt(oT[:, c, :], uT[:, c, :], zT[:, c, :], MUL), "oT_ready")
            mod_rows(1)

            def split(v, high, low, ready):
                run(nc.vector.tensor_copy(high, v))
                run(tt(low, v, high, SUB), ready)

            def split_panel(n):
                panel_arrived(dve, late[n])
                for j in last_users(LATE + n, ((3 + n % 2) * PANEL, (4 + n % 2) * PANEL)):
                    multiplied(dve, last_turn[panels[j]])
                split(panel(late[n], PANEL, 1), panel_high(late[n], PANEL, 1), panel_low(late[n], PANEL, 1), "w_split")

            def keys_and_scores(h):
                ks = slice(128 * h, 128 * h + 128)
                if h:
                    multiplied(dve, ("kvp", h - 1))
                    multiplied(dve, ("kvs", h - 1, 3))
                for t in range(2):
                    run(ts(kd[:, t, :], qk[:, 1, t, ks], rc[:, R_KD + HEADS * t + h:R_KD + HEADS * t + h + 1], None, MUL), "kd_ready")
                run(tt(kz, bc(qk[:, 1, 2, ks], 1, STREAMS),
                       bc(rc[:, R_ZM + STREAMS * h:R_ZM + STREAMS * h + STREAMS], 2, 128), MUL), "kz_ready")
                o = multiplied(dve, ("s", h))
                dve.wait_ge(S[f"mask_in{h % 2}"], 16 * (h // 2 + 1))
                if h >= 2:
                    multiplied(dve, ("oB", h - 2))
                run(tt(sT[:, h % 2, :], o[:, :], msk[:, h % 2, :], MUL), frees=("s", h))

            def retention(h):
                lg_ = float(np.log(1.0 - 2.0 ** (-5.0 - h)))
                o = multiplied(dve, ("kvp", h))
                if h:
                    dve.wait_ge(S["kv_out"], 16 * h)
                run(nc.vector.tensor_copy(kvo, o[:, 0:DV]), frees=("kvp", h))
                if h + 1 < HEADS:
                    keys_and_scores(h + 1)
                multiplied(dve, ("oB", h))
                for b2 in range(4):
                    o = multiplied(dve, ("kvs", h, b2))
                    st = s0[(2 * h + b2 // 2) % 3][:, 2 * (b2 % 2):2 * (b2 % 2) + 2, :]
                    run(stt(st, st, float(np.exp(lg_ * FRAMES)), o.rearrange("p (b d) -> p b d", b=2), MUL, ADD),
                        frees=("kvs", h, b2))
                dve.wait_ge(S["o_ssq"], T * (h + 1))
                run(ts(stat[:, 28:31], stat[:, 8 + T * h:11 + T * h], 1.0 / DV, EPS, MUL, ADD), "o_ms")
                dve.wait_ge(S["o_rstd"], h + 1)
                for t in range(T):
                    name = ("oA", h) if t < 2 else ("oB", h)
                    o = ps[turns[name][0]]
                    g = gg[:, t, DV * h:DV * h + DV]
                    run(stt(g, o[:, DV * (t % 2):DV * (t % 2) + DV], stat[:, 51 + t:52 + t], g, MUL, MUL), "og_ready")
                    if t:
                        run(ts(stat[:, 61:62], o[:, 0:1], 0.0, None, MUL), frees=name)

            dve.wait_ge(S["qx_zero"], 1)
            for h in range(HEADS):
                copied(dve, ("qT", h))
                qs = qT[:, h, SEQ:NTOK].rearrange("p (j r f) -> p j r f", r=2, f=FRAMES)
                xi = bc(rc[:, R_XI + FRAMES * h:R_XI + FRAMES * h + FRAMES], 1, 4)
                for r in range(2):
                    run(tt(qx[:, h, r::2, FRAMES * r:FRAMES * r + FRAMES], qs[:, :, r, :], xi, MUL), "qx_ready")
            keys_and_scores(0)
            retention(0)
            retention(1)
            multiplied(dve, ("glu", 3))
            dve.wait_ge(S["hf_out"], 16)
            split(nT, highT, nTlow, "nT_split")
            mod_rows(2)
            retention(2)
            split_panel(0)
            retention(3)
            split_panel(1)
            scales(3, V_N2, 2)
            for r, n in enumerate((3, 3, 2)):
                dve.wait_ge(S[f"s0_out{r}"], 16 * n)
            dve.wait_ge(S["kv_out"], 16 * HEADS)
            split(oT, oThigh, oTlow, "oT_split")
            for n in range(2, 5):
                split_panel(n)
            multiplied(dve, ("in", 10, T - 1))
            for k in range(0, KD, 2):
                copied(dve, ("ogT", k))
                copied(dve, ("ogT", k + 1))
                split(ogT[:, k:k + 2, :], highT[:, k:k + 2, :], ogTlow[:, k:k + 2, :], "ogT_split")
            for hf in range(2):
                for t in range(T):
                    if (hf, t) == (0, 2):
                        split_panel(5)
                    o = multiplied(dve, ("ya", hf, t))
                    copied(dve, ("in", 7 + hf, t))
                    ga = gates[:, t, 512 * hf:512 * hf + 512]
                    run(tt(ga, ga, o[:, :], MUL), frees=("ya", hf, t))
            for hf in range(2):
                for t in range(T):
                    if t == 0:
                        split_panel(6 + hf)
                    o = multiplied(dve, ("yb", hf, t))
                    copied(dve, ("in", 9 + hf, t))
                    ga = gates[:, t, 512 * hf:512 * hf + 512]
                    gb = gates[:, t, 1024 + 512 * hf:1536 + 512 * hf]
                    run(tt(gb, gb, o[:, :], MUL), frees=("yb", hf, t))
                    run(tt(ga, ga, gb, ADD), "merged")
            for k in range(0, KD, 2):
                copied(dve, ("mT", k))
                copied(dve, ("mT", k + 1))
                split(nT[:, k:k + 2, :], highT[:, k:k + 2, :], nTlow[:, k:k + 2, :], "mT_split")
            split_panel(8)
            dve.wait_ge(S["x2_in"], 16 * T)
            for v in range(2):
                for hf in range(2):
                    copied(dve, ("g1", v, hf))
            for hf in range(2):
                for t in range(T):
                    o = multiplied(dve, ("wo", hf, t))
                    gb = gates[:, t, 1024 + 512 * hf:1536 + 512 * hf]
                    xs = x2[:, t, 512 * hf:512 * hf + 512]
                    run(tt(gb, gte[:, t // 2, 512 * hf:512 * hf + 512], o[:, :], MUL), frees=("wo", hf, t))
                    run(tt(xs, xs, gb, ADD), "x2_ready")
            dve.wait_ge(S["n2_ssq"], T)
            run(ts(stat[:, 32:35], stat[:, 24:27], 1.0 / D, EPS, MUL, ADD), "n2_ms")
            dve.wait_ge(S["n2_rstd"], 1)
            for t in range(T):
                run(ts(gg[:, t, :], x2[:, t, :], stat[:, 54 + t:55 + t], None, MUL), "xn2_ready")
            modulate("x2T", 3, 2)

            o = multiplied(dve, "logits")
            run(nc.vector.tensor_copy(lg.rearrange("p t e -> p (t e)"), o[:, 0:T * 36]), frees="logits")
            col = lambda v: v.unsqueeze(2)

            def first_largest(x, n, onehot, largest):
                w = tw[:, :, 0:n]
                run(tred(largest, x, AX.X, ALU.max))
                run(tt(w, x, bc(largest, 2, n), ALU.is_equal))
                rev = const[:, C_EI + 1:C_EI + 1 + n]
                run(tt(w, w, bc(rev, 1, T), MUL))
                run(ts(onehot, w, 0.0, 1000.0, ALU.is_equal, MUL))
                run(tt(w, w, onehot, ADD))
                run(tred(tm[:, 0, :], w, AX.X, ALU.min))
                run(tt(onehot, w, bc(tm[:, 0, :], 2, n), ALU.is_equal))

            run(nc.vector.memset(t1, 0.0))
            first_largest(lg[:, :, 0:GROUPS], GROUPS, goh, tm[:, 1, :])
            ein = e_in[:, 0:12].rearrange("p (t g) -> p t g", t=T)
            run(tt(ein, lg[:, :, 0:GROUPS], bc(tm[:, 1, :], 2, GROUPS), SUB), "e_in_ready")
            for t in range(T):
                run(tt(tg[:, t, :].rearrange("p (g e) -> p g e", g=GROUPS),
                       lg[:, t, GROUPS:36].rearrange("p (g e) -> p g e", g=GROUPS), bc(goh[:, t, :], 2, EXPERTS), MUL))
            run(tred(el, tg.rearrange("p t (g e) -> p t e g", g=GROUPS), AX.X, ADD))
            first_largest(el, EXPERTS, eoh[:, 0], tm[:, 1, :])
            run(stt(el2, eoh[:, 0], -1e30, el, MUL, ADD))
            run(nc.vector.tensor_copy(gw, tm[:, 1, :]))
            first_largest(el2, EXPERTS, eoh[:, 1], tm[:, 1, :])
            run(tt(e_in[:, 12:15], tm[:, 1, :], gw, SUB), "e_in_ready")
            for k in range(2):
                for t in range(T):
                    run(tt(foh[:, k, t, :].rearrange("p (g e) -> p g e", g=GROUPS),
                           bc(goh[:, t, :], 2, EXPERTS), bc(eoh[:, k, t, :], 1, GROUPS), MUL))
            run(tt(sel, foh[:, 0], foh[:, 1], ADD), "sel_ready")
            for k in range(2):
                run(tt(tg, foh[:, k], bc(const[:, C_EB:C_EB + NEXP], 1, T), MUL))
                run(tred(brow[:, k, :], tg, AX.X, ADD))
            dve.wait_ge(S["e_out_ready"], 1)
            run(tred(gw, e_out[:, 0:12].rearrange("p (t g) -> p t g", t=T), AX.X, ADD))
            run(nc.vector.reciprocal(gw, gw))
            run(ts(tm[:, 0, :], e_out[:, 12:15], 1.0, None, ADD))
            run(nc.vector.reciprocal(tm[:, 0, :], tm[:, 0, :]))
            run(tt(wk[:, 0, :], tm[:, 0, :], gw, MUL))
            run(tt(wk[:, 1, :], wk[:, 0, :], e_out[:, 12:15], MUL))
            dve.wait_ge(S["rec_in"], 16)
            for k in range(2):
                run(nc.vector.tensor_copy(recf[:, :, k, 2], wk[:, k, :]), "rec_ready")
            o = multiplied(dve, "rank")
            for k in range(2):
                run(tt(tg.rearrange("p t e -> p (t e)"), foh[:, k].rearrange("p t e -> p (t e)"), o[:, 0:T * NEXP], MUL))
                run(tred(rk[:, k, :], tg, AX.X, ADD))
            run(ts(stat[:, 61:62], o[:, 0:1], 0.0, None, MUL), frees="rank")
            rk6, rows6 = rk.rearrange("p k t -> p (k t)"), rowf.rearrange("p k t -> p (k t)")
            np6, br6 = npass.rearrange("p k t -> p (k t)"), brow.rearrange("p k t -> p (k t)")
            p56 = ps5.rearrange("p k t j -> p (k t) j")
            run(tt(p56, bc(rk6, 2, 5), bc(const[:, C_PT:C_PT + 5], 1, 6), ALU.is_ge))
            run(tred(np6, p56, AX.X, ADD))
            run(tred(npcol[:, 0:1], np6, AX.X, ALU.max), "np_col")
            run(stt(rows6, rk6, float(PAIRS), br6, MUL, ADD))
            run(stt(rows6, np6, float(PAIRS * CAP), rows6, MUL, ADD))
            run(nc.vector.tensor_copy(rowi, rowf), "rows_ready")
            o = multiplied(dve, "np")
            run(tred(npcol[0:1, 1:2], o[0:1, 0:128], AX.X, ALU.max), frees="np")
            run(ts(npi[0:1, 0:1], npcol[0:1, 1:2], 1.0, None, ADD), "np_ready")
            passes = dve.value_load(npi[0:1, 0:1], min_val=1, max_val=MAXPASS)

            def pair(t, u, first=False):
                i = 2 * t + u
                dve.wait_ge(S["silu_ready"], i + 1)
                tt(hs[:, u, :], hs[:, u, :], ps[2 + u][:, FF:2 * FF], MUL).then_inc(S["hs_ready"], 1)
                dve.wait_ge(S["hTp_done"], i + 1)
                if not first:
                    dve.wait_ge(S["y_done"], i - 1)
                nc.vector.tensor_copy(hT[:, u].rearrange("p k s -> p (k s)"), ps[4][:, 0:FF]).then_inc(S["hT_ready"], 1)

            pair(0, 0, True)
            pair(0, 1, True)
            with dve.Fori(1, PAIRS // 2) as t:
                pair(t, 0)
                pair(t, 1)
            with dve.If(passes > 1):
                with dve.Fori(PAIRS // 2, passes * (PAIRS // 2)) as t:
                    pair(t, 0)
                    pair(t, 1)
            for v in range(2):
                for hf in range(2):
                    copied(dve, ("g2", v, hf))
            dve.wait_ge(S["fn_in"], 16)
            for t in range(T):
                dve.wait_ge(S[f"ys_in{t}"], 16)
                y = ys[:, t, 0, :]
                run(tt(y, y, ys[:, t, 1, :], ADD))
                run(tt(y, y, gte[:, t // 2, :], MUL))
                run(tt(x2[:, t, :], x2[:, t, :], y, ADD), "x3_ready")
            for t in range(T):
                dve.wait_ge(S["y3_ssq"], t + 1)
                run(ts(stat[:, 44 + t:45 + t], stat[:, 40 + t:41 + t], 1.0 / D, EPS, MUL, ADD), "y3_ms")
            for t in range(T):
                dve.wait_ge(S["y3_rstd"], t + 1)
                run(stt(yout[:, t, :], x2[:, t, :], stat[:, 57 + t:58 + t], fnorm, MUL, MUL), "yout_ready")

        @block.gpsimd
        def _(pool):
            run = Own(pool, pool_own)
            tt = nc.gpsimd.tensor_tensor

            def bc(v, axis, n):
                v = v.unsqueeze(axis)
                shape = list(v.shape)
                shape[axis] = n
                return v.broadcast_to(shape)

            pool.wait_ge(S["x_in"], 16 * T)
            pool.dma_start(meta_d, A["c_empty"]).then_inc(S["empty_out"], 16)
            run(nc.gpsimd.memset(btp, 0.0), "zeros_ready")
            half = const[:, C_HALF:C_HALF + 3]
            pool.wait_ge(S["const_in"], 16)
            pool.wait_ge(S["x_ms"], 1)
            run(tt(stat[:, 48:51], stat[:, 4:7], half, ALU.pow), "x_rstd")
            pool.wait_ge(S["rotation_ready"], 1)
            pre, pim = pw[:, 0], pw[:, 1]
            cpy = nc.gpsimd.tensor_copy
            run(nc.gpsimd.memset(pre[:, :, 16:40], 1.0))
            run(nc.gpsimd.memset(pim[:, :, 16:40], 0.0))
            run(cpy(pre[:, :, 0], disc[:, 6, :]))
            run(cpy(pim[:, :, 0], disc[:, 5, :]))

            def doubled(o, n):
                cr, ci = pre[:, :, o + n - 1:o + n].broadcast_to([128, NST, n]), pim[:, :, o + n - 1:o + n].broadcast_to([128, NST, n])
                ar, ai = pre[:, :, o:o + n], pim[:, :, o:o + n]
                ta, tb = ptmp[:, 0, :, 0:n], ptmp[:, 1, :, 0:n]
                run(tt(ta, ar, cr, MUL))
                run(tt(tb, ai, ci, MUL))
                m = min(n, (16 if o == 0 else 15) - n)
                run(tt(pre[:, :, o + n:o + n + m], ta[:, :, 0:m], tb[:, :, 0:m], SUB))
                run(tt(ta, ar, ci, MUL))
                run(tt(tb, ai, cr, MUL))
                run(tt(pim[:, :, o + n:o + n + m], ta[:, :, 0:m], tb[:, :, 0:m], ADD))

            for n in (1, 2, 4, 8):
                doubled(0, n)
            run(cpy(pre[:, :, 17], pre[:, :, 15]))
            run(cpy(pim[:, :, 17], pim[:, :, 15]))
            for n in (1, 2, 4, 8):
                doubled(17, n)
            pool.wait_ge(S["silu_c"], 1)
            for a in range(NST // 2):
                if a >= 2:
                    pool.wait_ge(S["h_ready"], 4 * (a - 1))
                tmp = rtmp.rearrange("p i (a b) -> p i a b", b=16)
                for i in range(2):
                    n = 2 * a + i
                    tv = [bc(pw[:, r, n, 16:40], 2, 16) for r in range(2)]
                    bv = [bc(pw[:, r, n, 0:16], 1, 24) for r in range(2)]
                    dst = [rot[:, a % 2, r, i, :].rearrange("p (a b) -> p a b", b=16) for r in range(2)]
                    for r, op in ((0, SUB), (1, ADD)):
                        run(tt(tmp[:, 0], tv[0], bv[r], MUL))
                        run(tt(tmp[:, 1], tv[1], bv[1 - r], MUL))
                        run(tt(dst[r], tmp[:, 0], tmp[:, 1], op), "rot_ready" if i else None)
            copied(pool, ("ada", 0))
            pool.dma_start(adab, A["b_ada"][1, :, :]).then_inc(S["adab_later_in"], 16)
            copied(pool, ("y", 3))
            pool.wait_ge(S["h_copied"], 2 * NST)
            for h in range(2):
                pool.dma_start(msk[:, h, :], A["c_mask"][h, :, :]).then_inc(S[f"mask_in{h}"], 16)

            def states_in(n):
                pool.dma_start(s0[n % 3], A["s0"][n // 2, :, 4 * (n % 2):4 * (n % 2) + 4, :]).then_inc(S[f"s0_in{n % 3}"], 16)

            states_in(0)
            states_in(1)
            pool.wait_ge(S["hf_out"], 16)
            states_in(2)
            pool.wait_ge(S["rope_done"], 4)
            run(nc.gpsimd.memset(qx, 0.0), "qx_zero")
            pool.wait_ge(S["adab_later_in"], 16)
            copied(pool, ("ada", 1))
            pool.dma_start(adab, A["b_ada"][2, :, :]).then_inc(S["adab_later_in"], 16)
            for h in range(HEADS):
                copied(pool, ("kvp", h))
                if h + 2 < HEADS:
                    copied(pool, ("s", h))
                    pool.dma_start(msk[:, h % 2, :], A["c_mask"][h + 2, :, :]).then_inc(S[f"mask_in{h % 2}"], 16)
                pool.dma_start(A["o_retp"][h, :, :], kvo).then_inc(S["kv_out"], 16)
                for n in (2 * h, 2 * h + 1):
                    copied(pool, ("kvs", h, 2 * (n % 2) + 1))
                    pool.dma_start(A["o_rets"][h, :, 4 * (n % 2):4 * (n % 2) + 4, :], s0[n % 3]).then_inc(S[f"s0_out{n % 3}"], 16)
                for n in (2 * h + 3, 2 * h + 4):
                    if n < 2 * HEADS:
                        pool.wait_ge(S[f"s0_out{n % 3}"], 16 * (n // 3))
                        states_in(n)
                pool.wait_ge(S["o_ms"], h + 1)
                if h:
                    pool.wait_ge(S["og_ready"], T * h)
                run(tt(stat[:, 51:54], stat[:, 28:31], half, ALU.pow), "o_rstd")
            for r, n in enumerate((3, 3, 2)):
                pool.wait_ge(S[f"s0_out{r}"], 16 * n)
            pool.wait_ge(S["kv_out"], 16 * HEADS)
            pool.wait_ge(S["og_ready"], T * HEADS)
            for t in range(T):
                pool.dma_start(x2[:, t, :], A["x"][t, :, :]).then_inc(S["x2_in"], 16)
            pool.dma_start(spread, A["c_spread"]).then_inc(S["spread_in"], 16)
            pool.wait_ge(S["n2_ms"], 1)
            run(tt(stat[:, 54:57], stat[:, 32:35], half, ALU.pow), "n2_rstd")
            pool.dma_start(fnorm, A["final_norm"].partition_broadcast(128)).then_inc(S["fn_in"], 16)
            pool.wait_ge(S["empty_out"], 16)
            pool.wait_ge(S["x2_ready"], 6)
            run(nc.gpsimd.memset(xg, 0.0), "xg_zero")
            pool.wait_ge(S["rec_ready"], 2)
            pool.wait_ge(S["rows_ready"], 1)
            ind = bass.IndirectOffsetOnAxis
            for k in range(2):
                for t in range(T):
                    nc.gpsimd.indirect_dma_start(out=meta_d, out_offset=ind(ap=rowi[:, k, t:t + 1], axis=0),
                                                 in_=rec[:, t, k, :], in_offset=None,
                                                 bounds_check=MAXPASS * 128 * PAIRS - 1, oob_is_err=False)\
                        .then_inc(S["recs_out"], 16)
            pool.wait_ge(S["recs_out"], 96)
            pool.dma_start(metai.rearrange("p (a e) w -> p a (e w)", a=MAXPASS),
                           meta_d.rearrange("(a s e) w -> s a (e w)", a=MAXPASS, s=128)).then_inc(S["meta_in"], 16)
            pool.wait_ge(S["meta_in"], 16)
            pool.wait_ge(S["n2_out"], 16 * T)
            pool.wait_ge(S["np_ready"], 1)
            passes = pool.value_load(npi[0:1, 0:1], min_val=1, max_val=MAXPASS)

            def gather(t, u, first=False):
                i = 2 * t + u
                if not first:
                    pool.wait_ge(S["tr_done"], i - 1)
                pool.wait_ge(S["meta_in"], 16)
                nc.gpsimd.tensor_copy(gidx[:, u, :], metai[:, bass.ds(i, 1), 0]).then_inc(S["gidx_copied"], 1)
                pool.wait_ge(S["gidx_copied"], i + 1)
                pool.nop(nofuse=True)
                nc.gpsimd.indirect_dma_start(out=xg[:, u, :], out_offset=None, in_=n2_d,
                                             in_offset=ind(ap=gidx[:, u, 0:1], axis=0),
                                             bounds_check=NTOK - 1, oob_is_err=False).then_inc(S[f"gathered{u}"], 16)

            def scatter(t, u, first=False):
                i = 2 * t + u
                if not first:
                    pool.wait_ge(S[f"scattered{u}"], 16 * t)
                pool.wait_ge(S["meta_in"], 16)
                nc.gpsimd.tensor_copy(sidx[:, u, :], metai[:, bass.ds(i, 1), 1]).then_inc(S["sidx_copied"], 1)
                pool.wait_ge(S["sidx_copied"], i + 1)
                pool.wait_ge(S["y_copied"], 2 * i + 2)
                pool.nop(nofuse=True)
                nc.gpsimd.indirect_dma_start(out=y_d, out_offset=ind(ap=sidx[:, u, 0:1], axis=0),
                                             in_=yb[:, u, :], in_offset=None,
                                             bounds_check=2 * NTOK - 1, oob_is_err=False).then_inc(S[f"scattered{u}"], 16)

            gather(0, 0, True)
            gather(0, 1, True)
            gather(1, 0)
            gather(1, 1)
            scatter(0, 0, True)
            gather(2, 0)
            scatter(0, 1, True)
            gather(2, 1)
            scatter(1, 0)
            with pool.Fori(2, PAIRS // 2 - 1) as t:
                gather(t + 1, 0)
                scatter(t - 1, 1)
                gather(t + 1, 1)
                scatter(t, 0)
            scatter(PAIRS // 2 - 2, 1)
            scatter(PAIRS // 2 - 1, 0)
            scatter(PAIRS // 2 - 1, 1)
            for u in range(2):
                pool.wait_ge(S[f"scattered{u}"], 16 * (PAIRS // 2))
            with pool.If(passes > 1):
                with pool.Fori(PAIRS // 2, passes * (PAIRS // 2)) as t:
                    for u in range(2):
                        gather(t, u)
                        scatter(t, u)
                for u in range(2):
                    pool.wait_ge(S[f"scattered{u}"], 16 * (PAIRS // 2) * passes)
            for t in range(T):
                pool.dma_start(ys[:, t], y_d.rearrange("(k t p) d -> t p k d", k=2, t=T)[t]).then_inc(S[f"ys_in{t}"], 16)
            for t in range(T):
                pool.wait_ge(S["y3_ms"], t + 1)
                run(tt(stat[:, 57 + t:58 + t], stat[:, 44 + t:45 + t], half[:, 0:1], ALU.pow), "y3_rstd")


def kernel(**inputs):
    import concourse.bacc as bacc
    from concourse.bass_utils import run_bass_kernel_spmd as run

    g = {k: np.asarray(v) for k, v in inputs.items()}
    C = np.ascontiguousarray
    l = 0
    G, P, J = 32, 64, 16

    def rows(w, kt, n):
        return w.reshape(kt, 128, n).transpose(1, 0, 2).reshape(128, kt * n)

    def panels(w, kt, width):
        n = w.shape[1] // width
        return C(w.reshape(kt, 128, n, width).transpose(2, 1, 0, 3).reshape(n, 128, kt * width))

    arrays = {}
    arrays["x"] = C(np.concatenate([g["x_prompt"].reshape(-1, D), g["x_sample"].reshape(-1, D)]).reshape(T, 128, D))
    cond = np.zeros((32, D), np.float32)
    cond[0] = g["c_prompt"][0]
    cond[1:NCOND] = g["c_sample"]
    arrays["condT"] = C(cond.T.reshape(KD, 128, 32).transpose(1, 0, 2).reshape(128, -1))
    arrays["p_ada"] = C(g["w_ada"][l].reshape(4, 2, 128, 3, 2048).transpose(3, 0, 2, 1, 4).reshape(12, 128, -1))
    arrays["p_in"] = panels(g["w_in"][l], KD, 512)
    arrays["p_glu"] = panels(g["s5_w_glu"][l], 4, 512)
    arrays["p_s5"] = panels(g["w_s5_out"][l], 4, 1024)
    arrays["p_ret"] = panels(g["w_ret_out"][l], KD, 512)
    arrays["p_out"] = panels(g["w_out"][l], KD, 512)
    arrays["b_ada"] = C(np.repeat(g["b_ada"][l].reshape(3, 4, 1, 512), 32, 2).reshape(3, 128, 512))
    by_state = lambda a: a.reshape(NST, 128).T
    by_chan = lambda a: a.reshape(-1, 128).T
    v = np.zeros((128, V_N), np.float32)
    v[:, V_DT:V_DT + NST] = by_state(np.repeat(g["s5_log_dt"][l][:, None], P, 1))
    v[:, V_ARE:V_ARE + NST] = by_state(g["s5_a_re"][l])
    v[:, V_AIM:V_AIM + NST] = by_state(g["s5_a_im"][l])
    v[:, V_N1:V_N1 + KD] = by_chan(g["norm1"][l])
    v[:, V_N2:V_N2 + KD] = by_chan(g["norm2"][l])
    v[:, V_D:V_D + 4] = by_chan(g["s5_d"][l])
    v[:, V_BG:V_BG + 4] = by_chan(g["s5_b_glu"][l])
    v[0:GROUPS, V_BR] = g["b_rg"][l]
    v[GROUPS:36, V_BR] = g["b_re"][l].reshape(-1)
    arrays["vecs"] = v
    bb = np.zeros((128, 2, NST, 32), np.float32)
    ct = np.zeros((128, 2, NST, 32), np.float32)
    for r, (bn, cn) in enumerate((("s5_b_re", "s5_c_re"), ("s5_b_im", "s5_c_im"))):
        b = g[bn][l].reshape(NST, 2, P, J)
        c = g[cn][l].reshape(NST, 2, J, P)
        for par in range(2):
            bb[P * par:P * par + P, r, :, J * par:J * par + J] = b[:, par].transpose(1, 0, 2)
            ct[P * par:P * par + P, r, :, J * par:J * par + J] = c[:, par].transpose(2, 0, 1)
    arrays["bb"] = bb.reshape(128, -1)
    arrays["ct"] = ct.reshape(128, -1)
    h0 = np.stack([g[n][l].reshape(STREAMS, NST, 128).transpose(2, 1, 0) for n in ("state_s5_re", "state_s5_im")], 1)
    arrays["h0"] = C(h0.reshape(128, -1))
    arrays["s0"] = C(g["state_ret"][l].transpose(1, 2, 0, 3))
    wr = np.concatenate([g["w_rg"][l], g["w_re"][l].transpose(1, 0, 2).reshape(D, NEXP)], 1)
    arrays["w_router"] = C(rows(wr, KD, 36))
    w13 = np.concatenate([g["w1"][l].reshape(NEXP, KD, 128, FF), g["w3"][l].reshape(NEXP, KD, 128, FF)], 3)
    w13 = w13.transpose(0, 2, 1, 3).reshape(NEXP, 128, -1)
    w2 = g["w2"][l].reshape(NEXP, 2, 128, D).transpose(0, 2, 1, 3).reshape(NEXP, 128, -1)
    arrays["p_up"] = C(w13.reshape(PAIRS, 2, 128, -1).transpose(0, 2, 1, 3))
    arrays["p_down"] = C(w2.reshape(PAIRS, 2, 128, -1).transpose(0, 2, 1, 3))
    arrays["final_norm"] = C(g["final_norm"].reshape(-1))
    arrays.update({k: C(a) for k, a in shape_constants().items()})

    nc = bacc.Bacc("TRN2", target_bir_lowering=False, num_devices=1)
    A = {}
    for name, a in arrays.items():
        A[name] = nc.dram_tensor(f"in_{name}", a.shape, mybir.dt.from_np(a.dtype), kind="ExternalInput").ap()
    outs = {"o_y": (T, 128, D), "o_s5": (128, 2 * NST * NCOND), "o_retp": (HEADS, DK, DV), "o_rets": (HEADS, DK, STREAMS, DV)}
    for name, shape in outs.items():
        A[name] = nc.dram_tensor(f"out_{name}", shape, mybir.dt.float32, kind="ExternalOutput").ap()
    build(nc, A)
    r = run(nc, [{f"in_{k}": a for k, a in arrays.items()}], core_ids=[0]).results[0]
    y = r["out_o_y"].reshape(NTOK, D)
    s5 = r["out_o_s5"].reshape(128, 2, NST, NCOND).transpose(1, 3, 2, 0).reshape(2, NCOND, G, P)
    rp = r["out_o_retp"].reshape(1, 1, HEADS, DK, DV)
    rs = r["out_o_rets"].transpose(2, 0, 1, 3).reshape(1, STREAMS, HEADS, DK, DV)
    return (C(y[:SEQ].reshape(1, SEQ, D)), C(y[SEQ:].reshape(STREAMS, FRAMES, D)),
            C(s5[0, 0:1][None]), C(s5[1, 0:1][None]), C(rp), C(s5[0, 1:][None]), C(s5[1, 1:][None]), C(rs))
```

```python
import numpy as np
import concourse.bass as bass
from concourse import mybir
from contextlib import ExitStack

D = 1024
SEQ = 256
STREAMS = 8
FRAMES = 16
T = 3
NTOK = T * 128
KD = D // 128
S5W = 512
NST = 16
HEADS = 4
DK = 128
DV = 256
GROUPS = 4
EXPERTS = 8
NEXP = GROUPS * EXPERTS
FF = 256
EPS = 1e-6
NCOND = 1 + STREAMS
CHUNK = 64
PAST = 256

CAP = 64
PAIRS = NEXP // 2
MAXPASS = NTOK // CAP
META = 3
NO_ROW = 4096

V_DT, V_ARE, V_AIM, V_N1, V_N2, V_D, V_BG, V_BR = 0, 16, 32, 48, 56, 64, 68, 72
V_N = 73
C_ID, C_UP, C_ONE, C_IOTA, C_PAR, C_PAIR, C_REV, C_PT, C_HALF = 0, 128, 256, 384, 512, 544, 576, 608, 613
C_N = 616
R_ROPE, R_XI, R_KD, R_ZM = 0, 768, 832, 840
R_N = 872


def shape_constants():
    f = np.float32
    p = np.arange(128)
    c = np.zeros((128, C_N), f)
    c[:, C_ID:C_ID + 128] = np.eye(128)
    c[:, C_UP:C_UP + 128] = p[:, None] < p[None, :]
    c[:, C_ONE:C_ONE + 128] = 1.0
    e = np.arange(NEXP)
    c[:, C_IOTA:C_IOTA + 128] = p
    c[:, C_PAR:C_PAR + 32] = CAP * (e % 2)
    c[:, C_PAIR:C_PAIR + 32] = e // 2
    c[:, C_REV:C_REV + 32] = NEXP - e
    c[:, C_PT:C_PT + 5] = CAP * np.arange(1, MAXPASS)
    c[:, C_HALF:C_HALF + 3] = -0.5
    stream = [np.zeros(128, int), np.zeros(128, int), p // FRAMES + 1]
    spread = np.zeros((128, 4, 2, 128), f)
    for j in range(4):
        for v, s in ((0, stream[0]), (1, stream[2])):
            spread[32 * j + s, j, v, p] = 1.0
    pos = np.stack([p, p + 128, PAST + p % FRAMES], 1).astype(f)
    theta = (1.0 / (10000.0 ** np.linspace(0.0, 1.0, DK // 2, dtype=f))).astype(f)
    ang = (pos[:, :, None] * theta).astype(f)
    r = np.zeros((128, R_N), f)
    s = f(DK ** -0.5)
    rope = np.stack([np.cos(ang), np.sin(ang), np.cos(ang) * s, np.sin(ang) * s], 2)
    r[:, R_ROPE:R_ROPE + 768] = rope.reshape(128, -1)
    lg = np.log(1.0 - 2.0 ** (-5.0 - np.arange(HEADS)))
    r[:, R_XI:R_XI + 64] = np.exp(lg[:, None] * (np.arange(FRAMES) + 1)).reshape(-1)
    r[:, R_KD:R_KD + 8] = np.exp(lg[None, None] * (SEQ - 1.0 - np.stack([p, p + 128], 1)[:, :, None])).reshape(128, 8)
    own = (p // FRAMES)[:, None, None] == np.arange(STREAMS)[None, None]
    r[:, R_ZM:R_ZM + 32] = (own * np.exp(lg[None, :, None] * (FRAMES - 1.0 - p % FRAMES)[:, None, None])).reshape(128, 32)
    n = np.arange(SEQ)
    full = np.exp(lg[:, None, None] * np.abs(n[:, None] - n[None, :])) * (n[:, None] // CHUNK <= n[None, :] // CHUNK)
    same = np.exp(lg[:, None, None] * np.abs(p[:, None] - p[None, :])) * (p[:, None] // FRAMES == p[None, :] // FRAMES)
    mask = np.concatenate([full[:, 0:128, :], full[:, 128:256, 128:256], same], 2).astype(f)
    starts = np.ones((128, NTOK), f)
    starts[:, 0] = 0.0
    starts[:, SEQ::FRAMES] = 0.0
    rec = np.zeros((128, 2, T, META), f)
    for k in range(2):
        rec[:, k, :, 0] = p[:, None] + 128 * np.arange(T) - NO_ROW
        rec[:, k, :, 1] = rec[:, k, :, 0] + NTOK * k
    return {"c_keep": c, "c_spread": spread.reshape(128, -1), "c_ret": r, "c_mask": mask, "c_starts": starts,
            "c_rec": rec.reshape(128, -1)}


def build(nc, A):
    f32, i32, f32r = mybir.dt.float32, mybir.dt.int32, mybir.dt.float32r
    ALU, ACT, AX = mybir.AluOpType, mybir.ActivationFunctionType, mybir.AxisListType
    MUL, ADD, SUB = ALU.mult, ALU.add, ALU.subtract
    ctx = ExitStack()
    with ctx:
        def sem(name):
            return ctx.enter_context(nc.semaphore(name))

        WORDS = 53200
        WEIGHTS = 24576
        base = (nc.sbuf_base + 31) // 32 * 32
        mem = [ctx.enter_context(nc.sbuf_tensor("weights", [128, WEIGHTS], f32)),
               ctx.enter_context(nc.sbuf_tensor("working", [128, WORDS - WEIGHTS], f32))]

        def shaped(v, *shape):
            if len(shape) == 1:
                return v
            names = " ".join(f"d{i}" for i in range(len(shape)))
            return v.rearrange(f"p ({names}) -> p {names}", **{f"d{i}": s for i, s in enumerate(shape)})

        def at(off, *shape, dt=None):
            n = int(np.prod(shape))
            assert off + n <= WEIGHTS or WEIGHTS <= off and off + n <= WORDS, (off, shape)
            v = mem[0][:, off:off + n] if off < WEIGHTS else mem[1][:, off - WEIGHTS:off - WEIGHTS + n]
            if dt is not None:
                v = v.bitcast(dt)
            return shaped(v, *shape)

        def part_at(off, *shape):
            n = int(np.prod(shape))
            if (off, n) not in part_tensors:
                part_tensors[off, n] = nc.alloc_sbuf_tensor_at(f"parts{off}", [128, n], f32r, offset=base + 4 * off)
            return shaped(part_tensors[off, n][:, :], *shape)

        part_tensors = {}

        class Region:

            def __init__(self, start, end):
                self.next, self.end = start, end

            def __call__(self, *shape, dt=None):
                o = self.next
                self.next += int(np.prod(shape))
                assert self.next <= self.end, (self.next, self.end)
                return at(o, *shape, dt=dt)

        PANEL, RING = 4096, 5
        UP, DOWN = KD * 2 * FF, 2 * D
        assert WEIGHTS == 4 * (UP + DOWN)
        keep = Region(WEIGHTS, WORDS)
        const = keep(C_N)
        vecs = keep(76)
        condT = keep(KD, 32)
        modrow = keep(3, 512)
        scsh = keep(4, KD, NCOND)
        adab = keep(512)
        stat = keep(64)
        rec = keep(2, T, META)
        wr = keep(KD, 36)
        B0 = (keep.next + 7) // 8 * 8
        W0 = B0 + 12288
        nT = at(B0, KD, NTOK)
        qk = at(B0 + 3072, 2, T, 512)
        vv = at(B0 + 6144, T, 1024)
        gg = at(B0 + 9216, T, 1024)
        gates = at(B0 + 3072, T, 2048)
        x_in = at(B0 + 6144, T, D)
        bbraw = at(B0 + 9216, 2, NST, 32)
        bbar = at(B0 + 10240, 2, NST, 32)
        btmp = at(B0 + 11264, 2, NST, 32)
        sqj = at(B0 + 11264, 1024)
        early = Region(RING * PANEL, WEIGHTS)
        zT = early(4, NTOK)
        pw = early(2, NST, 40)
        ptmp = early(2, NST, 8)
        starts = early(NTOK)
        hfin = early(2, NST, NCOND)
        rc = at(WORDS - R_N, R_N)
        work = Region(W0, WORDS - R_N)
        uT = work(4, NTOK)
        rot = work(2, 2, 2, NTOK)
        rtmp = work(2, NTOK)
        m4 = work(4, NTOK)
        condraw = at(work.next - 4 * NTOK, KD, 32)
        hri = work(2, 2, NTOK)
        decay = work(2, NTOK)
        btp = work(2, 4, 128)
        ct = work(2, NST, 32)
        h0 = work(2, NST, STREAMS)
        disc = work(14, NST)
        oT = uT
        W1 = W0 + 1536
        ret = Region(W1, WORDS - R_N)
        qT = ret(HEADS, NTOK)
        kT = ret(HEADS, NTOK)
        rtm = at(ret.next, 4, T, HEADS, 64)
        qx = ret(HEADS, STREAMS, 32)
        sT = ret(2, 512)
        kz = ret(STREAMS, 128)
        kd = ret(2, 128)
        msk = ret(2, 512)
        s0a = ret(2, 4, DV)
        s0 = [s0a[:, 0], s0a[:, 1], at(RING * PANEL + 3072, 4, DV)]
        kvo = ret(DV)
        oj = ret(DV)
        highT = part_at(RING * PANEL, KD, NTOK)
        high1 = part_at(4 * PANEL, KD, NTOK)
        nTlow, oTlow, ogTlow = part_at(B0, KD, NTOK), part_at(W0, 4, NTOK), part_at(W1, KD, NTOK)
        out = Region(W1, WORDS)
        ogT = out(KD, NTOK)
        spread = out(4, 2, 128)
        oThigh = part_at(out.next, 4, NTOK)
        x2 = at(WORDS - 5 * D, T, D)
        gte = at(WORDS - 2 * D, 2, D)
        fnorm = at(B0 + 2048, D)
        route = Region(B0 + 3072, B0 + 6144)
        rtT = route(NTOK)
        lg = route(T, 36)
        e_in = route(15)
        e_out = route(15)
        goh = route(T, GROUPS)
        eoh = route(2, T, EXPERTS)
        el = route(T, EXPERTS)
        el2 = route(T, EXPERTS)
        tg = route(2, T, NEXP)
        tw = route(T, EXPERTS)
        big = route(3, T)
        nth = route(T)
        foh = route(2, T, NEXP)
        sel = route(T, NEXP)
        rk = route(2, T)
        ps5 = route(2, T, 5)
        npass = route(2, T)
        bslot = route(2, T)
        bpair = route(2, T)
        slot = route(2, T)
        column = route(2, T)
        soh = route(2 * T, 128)
        coh = route(2 * T, PAIRS)
        cval = route(2 * T, PAIRS, META)
        npcol = route(4)
        npi = route(4, dt=i32)
        gw = route(T)
        wk = route(2, T)
        metao = route.next
        metai = route(MAXPASS * PAIRS, META, dt=i32)
        metaf = at(metao, MAXPASS * PAIRS, META)
        gidx = route(2, 1, dt=i32)
        sidx = route(2, 1, dt=i32)
        gatecol = route(2, 1)
        moe = Region(B0 + 6144, B0 + 9216)
        xg = moe(2, D)
        hs = moe(2, FF)
        hT = moe(2, 2, 128)
        xgT = at(B0, 2, KD, 128)
        yb = at(B0 + 9216, 2, D)
        LATER = (MAXPASS - 1) * PAIRS
        coh2 = at(B0 + 9216, 2 * T, LATER)
        cval2 = at(B0 + 9216 + 2 * T * LATER, 2 * T, LATER, META)
        sq2 = at(W1, D)
        ys = at(0, T, 2, D)
        yout = at(6144, T, D)
        sq3 = at(9216, D)

        wup = at(0, 2, 2, UP)
        wdown = at(4 * UP, 2, 2, DOWN)
        wup2 = at(WORDS - 5 * D - 2 * UP, 2, UP)

        ps = [ctx.enter_context(nc.psum_tensor(f"bank{i}", [128, 512], f32)) for i in range(8)]

        n2_d = nc.dram_tensor("n2_rows", (NTOK, D), f32).ap()
        y_d = nc.dram_tensor("expert_rows", (2 * NTOK, D), f32).ap()

        full = [sem(f"bank{i}_full") for i in range(8)]
        free = [sem(f"bank{i}_free") for i in range(8)]
        act_own, dve_own, pool_own = sem("act_own"), sem("dve_own"), sem("pool_own")
        panel_in = [sem(f"panel_in{i}") for i in range(RING)]
        names = ("const_in cond_in vecs_in x_in starts_in bb_in ct_in h0_in adab_in adab_later_in wr_in rec_in ret_in mask_in0 mask_in1 "
                 "s0_in0 s0_in1 s0_in2 spread_in x2_in fn_in ys_in0 ys_in1 ys_in2 "
                 "silu_c x_ssq x_ms x_rstd xn_ready scales1 scales3 prompt_xT prompt_x2T disc_exp expin_ready ang_ready disc_sin rotation_ready zeros_ready "
                 "bbar_ready bt_copied decay_ready rot_ready h_ready y_read h_copied z_ready oT_ready rope_done "
                 "qx_zero qx_ready kd_ready kz_ready o_ssq o_ms o_rstd og_ready merged x2_ready "
                 "n2_ssq n2_ms n2_rstd xn2_ready e_in_ready e_out_ready sel_ready records_ready later_records cval_ready cval2_ready "
                 "np_ready xg_zero w_split w_split_rest w_high n1_high n1_split high_moved oT_split ogT_split mT_split up_in0 up_in1 spare_in down_in0 down_in1 gathered0 gathered1 scattered0 scattered1 rows_out tr_done "
                 "xgT_ready h_done silu_ready hs_ready hTp_done hT_ready y_done y_copied gate_copied gidx_copied sidx_copied x3_ready y_summed y3_ssq y3_ms "
                 "y3_rstd yout_ready hf_out kv_out s0_out0 s0_out1 s0_out2 n2_out  y_out").split()
        S = {n: sem(n) for n in names}
        tally = {}

        class Own:

            def __init__(self, eng, own):
                self.eng, self.own = eng, own

            def __call__(self, ins, ready=None, frees=None):
                if frees is not None:
                    b, n = turns[frees]
                    ins.then_inc(free[b], 1)
                    self.eng.wait_ge(free[b], n)
                    return
                s = S[ready] if ready else self.own
                key = ready or id(s)
                tally[key] = tally.get(key, 0) + 1
                ins.then_inc(s, 1)
                self.eng.wait_ge(s, tally[key])

        turns = {}
        uses = [0] * 8
        rotating = [0]

        def turn(name, bank=None):
            if bank is None:
                bank = (0, 1, 2, 3, 7)[rotating[0] % 5]
                rotating[0] += 1
            if uses[bank]:
                nc.tensor.wait_ge(free[bank], uses[bank])
            uses[bank] += 1
            turns[name] = (bank, uses[bank])
            return ps[bank]

        def filled(ins, name):
            ins.then_inc(full[turns[name][0]], 1)

        def multiplied(eng, name):
            b, n = turns[name]
            eng.wait_ge(full[b], n)
            return ps[b]

        def copied(eng, name):
            b, n = turns[name]
            eng.wait_ge(free[b], n)

        panels = ([("ada", 0, j) for j in range(4)] + [("in", p) for p in range(7)] + [("glu", 0)]
                  + [("ada", m, j) for m in (1, 2) for j in range(4)] + [("in", p) for p in range(7, 11)]
                  + [("s5", 0)] + [("ret", h) for h in range(2)] + [("out", h) for h in range(2)])
        panel_at = {p: i for i, p in enumerate(panels)}
        split_keys = [("in", p) for p in range(1, 7)] + panels[panels.index(("in", 7)):]
        place = ([0, 1, 2, 3] + [0] + [1, 2, 1, 2, 1, 2] + [1] + [3, 0, 2, 1] + [3, 0, 2, 1] + [4, 1, 2, 4, 1, 2, 4, 1, 2])
        high_place = {key: (3, 0)[n % 2] for n, key in enumerate(split_keys[:6])}
        high_place.update({key: (3, 0)[n % 2] for n, key in enumerate(split_keys[6:])})
        arrival = [place[:i].count(place[i]) + 1 for i in range(len(panels))]
        last_turn = {}
        src = {"ada": A["p_ada"], "in": A["p_in"], "glu": A["p_glu"], "s5": A["p_s5"], "ret": A["p_ret"], "out": A["p_out"]}

        def panel(key, kt, width):
            return at(place[panel_at[key]] * PANEL, kt, width)

        def panel_high(key, kt, width):
            return part_at(high_place[key] * PANEL, kt, width)

        def panel_low(key, kt, width):
            return part_at(place[panel_at[key]] * PANEL, kt, width)

        def panel_arrived(eng, key):
            i = panel_at[key]
            eng.wait_ge(panel_in[place[i]], 16 * arrival[i])

        def last_users(i, words=None):
            lo, hi = words or (place[i] * PANEL, (place[i] + 1) * PANEL)
            found = {}
            for j in range(i):
                for q in [place[j]] + ([high_place[panels[j]]] if panels[j] in high_place else []):
                    if q * PANEL < hi and (q + 1) * PANEL > lo:
                        found[q] = j
            return sorted(set(found.values()))

        def high_place_free(eng, key):
            q = high_place[key]
            for j in last_users(panel_at[key], (q * PANEL, (q + 1) * PANEL)):
                multiplied(eng, last_turn[panels[j]])

        block = ctx.enter_context(nc.Block())
        ident = const[:, C_ID:C_ID + 128]

        @block.tensor
        def _(pe):
            mm = nc.tensor.matmul

            def transposes(name, pieces, bank=None):
                o = turn(name, bank)
                for off, n, m, piece in pieces:
                    ins = nc.tensor.transpose(o[0:n, off:off + m], piece, ident[0:m, 0:m])
                filled(ins, name)

            def ada(m):
                o = turn(("ada", m))
                for k in range(KD):
                    key = ("ada", m, k // 2)
                    if k % 2 == 0:
                        panel_arrived(pe, key)
                        last_turn[key] = ("ada", m)
                    for j in range(4):
                        ins = mm(o[32 * j:32 * j + 32, :], condT[:, k, :],
                                 panel(key, 2, 2048)[:, k % 2, 512 * j:512 * j + 512], start=k == 0, stop=k == KD - 1)
                filled(ins, ("ada", m))

            def adaT(m):
                copied(pe, ("ada", m))
                transposes(("adaT", m), [(128 * c, 128, 128, modrow[:, m, 128 * c:128 * c + 128]) for c in range(4)])

            def split_gemm(name, key, t, high, low, kt, width=512, lo=0, ready=None):
                whi, wlo = panel_high(key, kt, width), panel_low(key, kt, width)
                n = split_keys.index(key)
                pe.wait_ge(S["w_split"], n + 1)
                if 1 <= n <= 5:
                    pe.wait_ge(S["w_split_rest"], n)
                o = turn(name)
                for k in range(kt):
                    if ready and k % 2 == 0:
                        pe.wait_ge(S[ready], k // 2 + 1)
                    for n, (x, w) in enumerate(((high, whi), (high, wlo), (low, whi))):
                        ins = mm(o[:, :], x[:, k, 128 * t:128 * t + 128], w[:, k, lo:lo + 512],
                                 start=k == 0 and n == 0, stop=k == kt - 1 and n == 2)
                filled(ins, name)
                last_turn[key] = name

            def chan_gemm(name, key, c, rhs, kt, of=None):
                wv = panel(key, kt, 512)
                o = turn(name)
                for k in range(kt):
                    if of:
                        copied(pe, (of, k))
                    ins = mm(o[:, 0:NTOK], wv[:, k, 128 * c:128 * c + 128], rhs[:, k, :], start=k == 0, stop=k == kt - 1)
                filled(ins, name)
                last_turn[key] = name

            def x_transposes(k, bank=None):
                transposes(("xT", k), [(128 * t, 128, 128, x_in[:, t, 128 * k:128 * k + 128]) for t in range(T)], bank)

            pe.wait_ge(S["const_in"], 16)
            pe.wait_ge(S["xn_ready"], T)
            for k in range(3):
                x_transposes(k, 4 + k)
            for k in range(3, 6):
                x_transposes(k)
            pe.wait_ge(S["silu_c"], 1)
            ada(0)
            adaT(0)
            for k in range(6, KD):
                x_transposes(k)
            panel_arrived(pe, ("in", 0))
            for c in range(4):
                chan_gemm(("u", c), ("in", 0), c, nT, KD, "xT" if c == 0 else None)

            def b_transposes(a):
                if a == 0:
                    pe.wait_ge(S["bbar_ready"], 2)
                transposes(("BT", a), [(128 * r, 128, 128, at(B0 + 10240 + 512 * r + 128 * a, 128)) for r in range(2)])

            def bu(i):
                a, q = divmod(i, 4)
                if q == 0:
                    copied(pe, ("u", a))
                    pe.wait_ge(S["bt_copied"], 8 * (a + 1))
                for r in range(2):
                    o = turn(("bu", i, r), 5 + r)
                    filled(mm(o[:, 0:NTOK], btp[:, r, q, :], uT[:, a, :], start=True, stop=True), ("bu", i, r))

            def y_sum(i):
                a, q = divmod(i, 4)
                pe.wait_ge(S["h_ready"], 2 * (i + 1))
                if q == 0:
                    turn(("y", a), 4)
                if i == 0:
                    pe.wait_ge(S["ct_in"], 16)
                mm(ps[4][32 * q:32 * q + 32, 0:NTOK], ct[:, 0, i, :], hri[:, i % 2, 0, :], start=True, stop=False)
                ins = mm(ps[4][32 * q:32 * q + 32, 0:NTOK], ct[:, 1, i, :], hri[:, i % 2, 1, :], start=False, stop=True)
                ins.then_inc(S["y_read"], 1)

            b_transposes(0)
            for j in range(18):
                if j < NST:
                    bu(j)
                    if j % 4 == 3 and j < NST - 1:
                        b_transposes(j // 4 + 1)
                key = ("in", 1 + j // 3)
                split_gemm((*key, j % 3), key, j % 3, high1, nTlow, KD, ready="n1_split")
                if j >= 2:
                    y_sum(j - 2)
            pe.wait_ge(S["z_ready"], 4)
            panel_arrived(pe, ("glu", 0))
            for c in range(4):
                chan_gemm(("glu", c), ("glu", 0), c, zT, 4)
            pe.wait_ge(S["rope_done"], 4)
            for r, n in ((0, "qT"), (1, "kT")):
                for h in range(HEADS):
                    transposes((n, h), [(128 * t, 128, 128, qk[:, r, t, 128 * h:128 * h + 128]) for t in range(T)])

            def scores(h):
                copied(pe, ("qT", h))
                copied(pe, ("kT", h))
                o = turn(("s", h))
                mm(o[:, 0:256], kT[:, h, 0:128], qT[:, h, 0:256], start=True, stop=True)
                mm(o[:, 256:384], kT[:, h, 128:256], qT[:, h, 128:256], start=True, stop=True)
                filled(mm(o[:, 384:512], kT[:, h, 256:384], qT[:, h, 256:384], start=True, stop=True), ("s", h))

            def head(h):
                lo = DV * h
                pe.wait_ge(S["kd_ready"], 2 * (h + 1))
                o = turn(("kvp", h))
                mm(o[:, 0:DV], kd[:, 0, :], vv[:, 0, lo:lo + DV], start=True, stop=False)
                filled(mm(o[:, 0:DV], kd[:, 1, :], vv[:, 1, lo:lo + DV], start=False, stop=True), ("kvp", h))
                pe.wait_ge(S["kz_ready"], h + 1)
                for b2 in range(4):
                    o = turn(("kvs", h, b2))
                    for r in range(2):
                        ins = mm(o[:, DV * r:DV * r + DV], kz[:, 2 * b2 + r, :], vv[:, 2, lo:lo + DV], start=True, stop=True)
                    filled(ins, ("kvs", h, b2))
                if h + 1 < HEADS:
                    scores(h + 1)
                copied(pe, ("s", h))
                o = turn(("oA", h), 5)
                mm(o[:, 0:DV], sT[:, h % 2, 0:128], vv[:, 0, lo:lo + DV], start=True, stop=True)
                mm(o[:, DV:2 * DV], sT[:, h % 2, 128:256], vv[:, 0, lo:lo + DV], start=True, stop=False)
                filled(mm(o[:, DV:2 * DV], sT[:, h % 2, 256:384], vv[:, 1, lo:lo + DV], start=False, stop=True), ("oA", h))
                o = turn(("oB", h), 6)
                mm(o[:, 0:DV], sT[:, h % 2, 384:512], vv[:, 2, lo:lo + DV], start=True, stop=False, skip_group_check=True)
                pe.wait_ge(S["qx_ready"], 2 * HEADS)
                for half in range(2):
                    n = 2 * h + half
                    pe.wait_ge(S[f"s0_in{n % 3}"], 16 * (n // 3 + 1))
                    for b in range(4):
                        b8 = 4 * half + b
                        j = 32 * (b8 // 2)
                        ins = mm(o[j:j + 32, 0:DV], qx[:, h, b8, :], s0[n % 3][:, b, :], start=False, stop=b8 == 7,
                                 skip_group_check=True)
                filled(ins, ("oB", h))

            scores(0)
            ada(1)
            head(0)
            adaT(1)
            head(1)
            ada(2)
            head(2)
            adaT(2)
            head(3)
            pe.wait_ge(S["high_moved"], 1)
            for p in range(7, 11):
                for t in range(T):
                    split_gemm(("in", p, t), ("in", p), t, highT, nTlow, KD)
            pe.wait_ge(S["og_ready"], T * HEADS)
            for k in range(KD):
                transposes(("ogT", k), [(128 * t, 128, 128, gg[:, t, 128 * k:128 * k + 128]) for t in range(T)])
            pe.wait_ge(S["oT_split"], 1)
            for hf in range(2):
                for t in range(T):
                    split_gemm(("ya", hf, t), ("s5", 0), t, oThigh, oTlow, 4, 1024, 512 * hf)
            for hf in range(2):
                for t in range(T):
                    split_gemm(("yb", hf, t), ("ret", hf), t, highT, ogTlow, KD, ready="ogT_split")

            def gate_rows(name, m):
                for v in range(2):
                    for hf in range(2):
                        o = turn((name, v, hf))
                        j = hf if m == 1 else 2 + hf
                        filled(mm(o[:, :], spread[:, j, v, :], modrow[:, m, :], start=True, stop=True), (name, v, hf))

            pe.wait_ge(S["spread_in"], 16)
            gate_rows("g1", 1)
            pe.wait_ge(S["merged"], 6)
            for k in range(KD):
                transposes(("mT", k), [(128 * t, 128, 128, gates[:, t, 128 * k:128 * k + 128]) for t in range(T)])
            for hf in range(2):
                for t in range(T):
                    split_gemm(("wo", hf, t), ("out", hf), t, highT, nTlow, KD, ready="mT_split")
            gate_rows("g2", 2)
            pe.wait_ge(S["xn2_ready"], T)
            for k in range(KD):
                transposes(("x2T", k), [(128 * t, 128, 128, gg[:, t, 128 * k:128 * k + 128]) for t in range(T)])
            pe.wait_ge(S["wr_in"], 16)
            o = turn("router")
            for k in range(KD):
                copied(pe, ("x2T", k))
                ins = mm(o[0:36, 0:NTOK], wr[:, k, :], nT[:, k, :], start=k == 0, stop=k == KD - 1)
            filled(ins, "router")
            for t in range(T):
                for hf in range(2):
                    transposes(("n2", t, hf), [(128 * c, 128, 128, nT[:, 4 * hf + c, 128 * t:128 * t + 128]) for c in range(4)])
                    if (t, hf) == (0, 0):
                        copied(pe, "router")
                        transposes("logits", [(36 * s, 128, 36, rtT[0:36, 128 * s:128 * s + 128]) for s in range(T)])
            pe.wait_ge(S["sel_ready"], 1)
            o = turn("rank")
            for t in range(T):
                for s in range(t + 1):
                    lhs = const[:, C_UP:C_UP + 128] if s == t else const[:, C_ONE:C_ONE + 128]
                    ins = mm(o[:, NEXP * t:NEXP * t + NEXP], lhs, sel[:, s, :], start=s == 0, stop=s == t)
            filled(ins, "rank")

            def records(name, ready, values, n, bank=None):
                pe.wait_ge(S[ready], 1)
                o = turn(name, bank)
                for j in range(2 * T):
                    ins = mm(o[:, 0:META * n], soh[:, j, :], values[:, j].rearrange("p c w -> p (c w)"),
                             start=j == 0, stop=j == 2 * T - 1)
                filled(ins, name)

            records("slots", "cval_ready", cval, PAIRS)
            for b in range(8):
                if uses[b]:
                    pe.wait_ge(free[b], uses[b])
            def rows_by_channel(t, u):
                i = 2 * t + u
                pe.wait_ge(S[f"gathered{u}"], 16 * t + 16)
                if not (isinstance(i, int) and i == 0):
                    pe.wait_ge(S["xgT_ready"], 2 * i)
                for k in range(KD):
                    ins = nc.tensor.transpose(ps[k // 4][:, 128 * (k % 4):128 * (k % 4) + 128],
                                              xg[:, u, 128 * k:128 * k + 128], ident)
                ins.then_inc(S["tr_done"], 1)

            def up(t, u, first=False, w=None):
                i = 2 * t + u
                if w is not None:
                    pe.wait_ge(S["spare_in"], 32)
                elif u == 0 and not first:
                    pe.wait_ge(S["up_in0"], 16 * t)
                else:
                    pe.wait_ge(S[f"up_in{u}"], 16 * t + 16)
                w = wup[:, u] if w is None else w
                pe.wait_ge(S["xgT_ready"], 2 * i + 2)
                if not first:
                    pe.wait_ge(S["hs_ready"], i - 1)
                for k in range(KD):
                    for e in range(2):
                        ins = mm(ps[2 + u][64 * e:64 * e + 64, :], xgT[:, u, k, 64 * e:64 * e + 64],
                                 w[:, e, 512 * k:512 * k + 512], start=k == 0, stop=k == KD - 1)
                ins.then_inc(S["h_done"], 1)

            def hidden_by_channel(t, u):
                i = 2 * t + u
                pe.wait_ge(S["hs_ready"], i + 1)
                if not (isinstance(i, int) and i == 0):
                    pe.wait_ge(S["hT_ready"], i)
                for k in range(2):
                    ins = nc.tensor.transpose(ps[4][:, 128 * k:128 * k + 128], hs[:, u, 128 * k:128 * k + 128], ident)
                ins.then_inc(S["hTp_done"], 1)

            def down(t, u):
                i = 2 * t + u
                pe.wait_ge(S[f"down_in{u}"], 16 * t + 16)
                pe.wait_ge(S["hT_ready"], i + 1)
                if not (isinstance(i, int) and i == 0):
                    pe.wait_ge(S["y_copied"], 2 * i)
                for hf in range(2):
                    for k in range(2):
                        for e in range(2):
                            o_ = 1024 * k + 512 * hf
                            ins = mm(ps[5 + hf][64 * e:64 * e + 64, :], hT[:, u, k, 64 * e:64 * e + 64],
                                     wdown[:, u, e, o_:o_ + 512], start=k == 0, stop=k == 1)
                ins.then_inc(S["y_done"], 1)

            LAST = PAIRS // 2 - 1
            rows_by_channel(0, 0)
            up(0, 0, True)
            records("slots2", "cval2_ready", cval2, LATER, 7)
            transposes("np", [(0, 1, 128, npcol[:, 0:1])], 7)
            rows_by_channel(0, 1)
            hidden_by_channel(0, 0)
            up(0, 1, True)

            def two_pairs(t, w=None):
                rows_by_channel(t, 0)
                down(t - 1, 0)
                hidden_by_channel(t - 1, 1)
                up(t, 0, w=w)
                rows_by_channel(t, 1)
                down(t - 1, 1)
                hidden_by_channel(t, 0)
                up(t, 1)

            two_pairs(1, wup2)
            with pe.Fori(2, PAIRS // 2) as t:
                two_pairs(t)
            down(LAST, 0)
            hidden_by_channel(LAST, 1)
            down(LAST, 1)
            pe.wait_ge(S["np_ready"], 1)
            passes = pe.value_load(npi[0:1, 0:1], min_val=1, max_val=MAXPASS)
            with pe.If(passes > 1):
                with pe.Fori(PAIRS // 2, passes * (PAIRS // 2)) as t:
                    for u in range(2):
                        rows_by_channel(t, u)
                        up(t, u)
                        hidden_by_channel(t, u)
                        down(t, u)

        @block.sync
        def _(sp):
            for t in range(T):
                sp.dma_start(x_in[:, t, :], A["x"][t, :, :]).then_inc(S["x_in"], 16)
            for i, key in enumerate(panels):
                if key == ("ada", 2, 2):
                    sp.wait_ge(S["s0_in0"], 16 * 2)
                if key == ("in", 8):
                    sp.wait_ge(S["s0_in1"], 16 * 3)
                for j in last_users(i):
                    multiplied(sp, last_turn[panels[j]])
                if key == ("in", 7):
                    sp.wait_ge(S["high_moved"], 1)
                n = 2048 if key[0] == "glu" else PANEL
                d = src[key[0]][4 * key[1] + key[2] if key[0] == "ada" else key[1], :, :]
                sp.dma_start(at(place[i] * PANEL, n), d).then_inc(panel_in[place[i]], 16)
                if key == ("in", 0):
                    sp.dma_start(bbraw, A["bb"]).then_inc(S["bb_in"], 16)
                    sp.dma_start(starts, A["c_starts"]).then_inc(S["starts_in"], 16)
                    sp.dma_start(h0, A["h0"]).then_inc(S["h0_in"], 16)
                    sp.dma_start(ct, A["ct"]).then_inc(S["ct_in"], 16)
                    sp.dma_start(wr, A["w_router"]).then_inc(S["wr_in"], 16)
                    sp.dma_start(rec, A["c_rec"]).then_inc(S["rec_in"], 16)
                    sp.dma_start(rc, A["c_ret"]).then_inc(S["ret_in"], 16)

            def free_place(lo, hi):
                for j in last_users(len(panels), (lo, hi)):
                    multiplied(sp, last_turn[panels[j]])

            for u in range(2):
                free_place(u * 2 * UP, (u + 1) * 2 * UP)
                sp.dma_start(wup[:, u], A["p_up"][u, :, :, :]).then_inc(S[f"up_in{u}"], 16)
                if u == 0:
                    sp.wait_ge(S["hf_out"], 16)
                free_place(4 * UP + u * 2 * DOWN, 4 * UP + (u + 1) * 2 * DOWN)
                sp.dma_start(wdown[:, u], A["p_down"][u, :, :, :]).then_inc(S[f"down_in{u}"], 16)

            def load(t, m, u):
                sp.wait_ge(S["h_done"], 2 * t + u - 1)
                sp.dma_start(wup[:, u], A["p_up"][2 * m + u, :, :, :]).then_inc(S[f"up_in{u}"], 16)
                sp.wait_ge(S["y_done"], 2 * t + u - 1)
                sp.dma_start(wdown[:, u], A["p_down"][2 * m + u, :, :, :]).then_inc(S[f"down_in{u}"], 16)

            multiplied(sp, ("g2", 1, 1))
            sp.wait_ge(S["n2_ssq"], T)
            sp.dma_start(wup2[:, 1], A["p_up"][2, :, 1, :]).then_inc(S["spare_in"], 16)
            sp.wait_ge(S["n2_out"], 16 * T)
            sp.dma_start(wup2[:, 0], A["p_up"][2, :, 0, :]).then_inc(S["spare_in"], 16)
            sp.wait_ge(S["h_done"], 1)
            sp.dma_start(wup[:, 0], A["p_up"][4, :, :, :]).then_inc(S["up_in0"], 16)
            sp.wait_ge(S["y_done"], 1)
            sp.dma_start(wdown[:, 0], A["p_down"][2, :, :, :]).then_inc(S["down_in0"], 16)
            load(1, 1, 1)
            sp.wait_ge(S["y_done"], 3)
            sp.dma_start(wdown[:, 0], A["p_down"][4, :, :, :]).then_inc(S["down_in0"], 16)
            load(2, 2, 1)
            with sp.Fori(3, PAIRS // 2) as t:
                load(t, t, 0)
                load(t, t, 1)
            sp.wait_ge(S["np_ready"], 1)
            passes = sp.value_load(npi[0:1, 0:1], min_val=1, max_val=MAXPASS)
            with sp.If(passes > 1):
                with sp.Fori(PAIRS // 2, passes * (PAIRS // 2)) as t:
                    load(t, t % (PAIRS // 2), 0)
                    load(t, t % (PAIRS // 2), 1)
            sp.wait_ge(S["rows_out"], 1)
            for t in range(T):
                sp.dma_start(ys[:, t], y_d.rearrange("(k t p) d -> t p k d", k=2, t=T)[t]).then_inc(S[f"ys_in{t}"], 16)

        @block.scalar
        def _(act):
            run = Own(act, act_own)
            A_ = nc.scalar.activation
            cp = nc.scalar.copy
            act.dma_start(vecs[:, 0:V_N], A["vecs"]).then_inc(S["vecs_in"], 16)
            act.dma_start(condraw, A["condT"]).then_inc(S["cond_in"], 16)
            act.dma_start(const, A["c_keep"]).then_inc(S["const_in"], 16)
            act.dma_start(adab, A["b_ada"][0, :, :]).then_inc(S["adab_in"], 16)
            act.wait_ge(S["cond_in"], 16)
            run(A_(condT, condraw, ACT.Silu), "silu_c")
            act.wait_ge(S["x_in"], 16 * T)
            for t in range(T):
                run(A_(sqj, x_in[:, t, :], ACT.Square, accum_out=stat[:, t:t + 1]), "x_ssq")
            act.wait_ge(S["vecs_in"], 16)
            run(A_(disc[:, 0, :], vecs[:, V_DT:V_DT + NST], ACT.Exp), "disc_exp")
            act.wait_ge(S["expin_ready"], 1)
            run(A_(disc[:, 2, :], disc[:, 1, :], ACT.Exp), "disc_exp")
            act.wait_ge(S["ang_ready"], 1)
            run(A_(disc[:, 5, :], disc[:, 4, :], ACT.Sin), "disc_sin")
            run(A_(disc[:, 6, :], disc[:, 4, :], ACT.Sin, scale=0.5), "disc_sin")

            def mod_columns(m):
                o = multiplied(act, ("adaT", m)).rearrange("p (c j s) -> p c j s", c=4, j=4)
                pieces = [(h, v, j) for h, v in {0: [(0, 0), (1, 1)], 1: [(1, 2)], 2: [(0, 3)]}[m] for j in range(2)]
                for n, (half, vec, j) in enumerate(pieces):
                    run(cp(scsh[:, vec, 4 * j:4 * j + 4, :], o[:, :, 2 * half + j, 0:NCOND]),
                        frees=("adaT", m) if n == len(pieces) - 1 else None)

            def modulate(name, sc, sh):
                act.wait_ge(S[f"scales{sc}"], 1)
                for k in range(KD):
                    o = multiplied(act, (name, k))
                    run(A_(nT[:, k, 0:SEQ], o[:, 0:SEQ], ACT.Identity, scale=scsh[:, sc, k, 0:1], bias=scsh[:, sh, k, 0:1]),
                        f"prompt_{name}")

            mod_columns(0)
            modulate("xT", 1, 0)

            def leading_parts(key):
                panel_arrived(act, key)
                high_place_free(act, key)
                run(cp(panel_high(key, PANEL, 1), panel(key, PANEL, 1)), "w_high")

            for k in range(KD):
                copied(act, ("xT", k))
            run(cp(high1, nT), "n1_high")
            leading_parts(("in", 1))
            for c in range(4):
                o = multiplied(act, ("u", c))
                run(cp(uT[:, c, :], o[:, 0:NTOK]), frees=("u", c))

            def bt_copy(a):
                if a == 0:
                    act.wait_ge(S["zeros_ready"], 1)
                else:
                    multiplied(act, ("bu", 4 * a - 1, 1))
                o = multiplied(act, ("BT", a))
                for r in range(2):
                    for q in range(4):
                        run(cp(btp[32 * q:32 * q + 32, r, q, :], o[32 * q:32 * q + 32, 128 * r:128 * r + 128]), "bt_copied")
                run(cp(stat[:, 60:61], o[:, 0:1]), frees=("BT", a))

            def decays(i):
                if i == 0:
                    act.wait_ge(S["starts_in"], 16)
                else:
                    act.wait_ge(S["h_ready"], 2 * i)
                run(A_(decay, starts.unsqueeze(1).broadcast_to([128, 2, NTOK]), ACT.Copy, scale=disc[:, 2, i:i + 1]), "decay_ready")

            def last_states(i):
                act.wait_ge(S["h_ready"], 2 * i + 2)
                for r in range(2):
                    run(cp(hfin[:, r, i, :], hri[:, i % 2, r, SEQ - 1::FRAMES]), "h_copied")

            bt_copy(0)
            for j in range(18):
                if j < NST:
                    decays(j)
                if j % 4 == 3 and j < NST - 1:
                    bt_copy(j // 4 + 1)
                p, t = 1 + j // 3, j % 3
                o = multiplied(act, ("in", p, t))
                if p <= 2:
                    run(cp(qk[:, p - 1, t, :], o[:, :]), frees=("in", p, t))
                elif p <= 4:
                    run(cp(vv[:, t, 512 * (p - 3):512 * (p - 3) + 512], o[:, :]), frees=("in", p, t))
                else:
                    run(A_(gg[:, t, 512 * (p - 5):512 * (p - 5) + 512], o[:, :], ACT.Silu), frees=("in", p, t))
                if t == 0 and p < 6:
                    leading_parts(("in", p + 1))
                if j < NST:
                    last_states(j)
            act.dma_start(A["o_s5"], hfin).then_inc(S["hf_out"], 16)
            for a in range(4):
                copied(act, ("y", a))
                run(A_(zT[:, a, :], zT[:, a, :], ACT.Gelu_apprx_tanh), "z_ready")
            for c in range(4):
                o = multiplied(act, ("glu", c))
                run(A_(uT[:, c, :], o[:, 0:NTOK], ACT.Sigmoid, bias=vecs[:, V_BG + c:V_BG + c + 1]), frees=("glu", c))
            for n, dst in (("qT", qT), ("kT", kT)):
                for h in range(HEADS):
                    o = multiplied(act, (n, h))
                    run(cp(dst[:, h, :], o[:, 0:NTOK]), frees=(n, h))

            act.wait_ge(S["oT_ready"], 4)
            act.wait_ge(S["hf_out"], 16)
            run(cp(highT, high1), "high_moved")

            def o_squares(h):
                for t in range(T):
                    o = multiplied(act, ("oA", h) if t < 2 else ("oB", h))
                    run(A_(oj, o[:, DV * (t % 2):DV * (t % 2) + DV], ACT.Square,
                           accum_out=stat[:, 8 + T * h + t:9 + T * h + t]), "o_ssq")

            o_squares(0)
            mod_columns(1)
            o_squares(1)
            o_squares(2)
            mod_columns(2)
            o_squares(3)
            act.wait_ge(S["og_ready"], T * HEADS)
            for p in range(7, 11):
                for t in range(T):
                    o = multiplied(act, ("in", p, t))
                    run(A_(gates[:, t, 512 * (p - 7):512 * (p - 7) + 512], o[:, :], ACT.Sigmoid), frees=("in", p, t))
            for k in range(KD):
                o = multiplied(act, ("ogT", k))
                run(cp(ogT[:, k, :], o[:, 0:NTOK]), frees=("ogT", k))
            for r, n in enumerate((3, 3, 2)):
                act.wait_ge(S[f"s0_out{r}"], 16 * n)
            act.wait_ge(S["kv_out"], 16 * HEADS)
            for v in range(2):
                for hf in range(2):
                    o = multiplied(act, ("g1", v, hf))
                    run(cp(gte[:, v, 512 * hf:512 * hf + 512], o[:, :]), frees=("g1", v, hf))
            for k in range(KD):
                o = multiplied(act, ("mT", k))
                run(cp(nT[:, k, :], o[:, 0:NTOK]), frees=("mT", k))
            act.wait_ge(S["x2_ready"], 6)
            for t in range(T):
                run(A_(sq2, x2[:, t, :], ACT.Square, accum_out=stat[:, 24 + t:25 + t]), "n2_ssq")
            for v in range(2):
                for hf in range(2):
                    o = multiplied(act, ("g2", v, hf))
                    run(cp(gte[:, v, 512 * hf:512 * hf + 512], o[:, :]), frees=("g2", v, hf))
            modulate("x2T", 3, 2)
            o = multiplied(act, "router")
            run(A_(rtT[0:36, :], o[0:36, 0:NTOK], ACT.Identity, bias=vecs[0:36, V_BR:V_BR + 1]), frees="router")
            for t in range(T):
                for hf in range(2):
                    o = multiplied(act, ("n2", t, hf))
                    run(cp(gg[:, t, 512 * hf:512 * hf + 512], o[:, :]), frees=("n2", t, hf))
                act.dma_start(n2_d[128 * t:128 * t + 128, :], gg[:, t, :]).then_inc(S["n2_out"], 16)
            act.wait_ge(S["e_in_ready"], 2)
            run(A_(e_out, e_in, ACT.Exp), "e_out_ready")
            act.wait_ge(S["n2_out"], 16 * T)

            def rows_copy(t, u, first=False):
                i = 2 * t + u
                act.wait_ge(S["tr_done"], i + 1)
                if not first:
                    act.wait_ge(S["h_done"], i - 1)
                for c in range(2):
                    cp(at(B0 + u * 1024 + 512 * c, 512), ps[c][:, :]).then_inc(S["xgT_ready"], 1)

            def silu(t, u, first=False):
                i = 2 * t + u
                act.wait_ge(S["h_done"], i + 1)
                if not first:
                    act.wait_ge(S["hTp_done"], i - 1)
                A_(hs[:, u, :], ps[2 + u][:, 0:FF], ACT.Silu).then_inc(S["silu_ready"], 1)
                if not first:
                    act.wait_ge(S["y_copied"], 2 * i - 2)
                cp(gatecol[:, u, :], metaf[:, bass.ds(i, 1), 2]).then_inc(S["gate_copied"], 1)

            def rows_out(t, u, first=False):
                i = 2 * t + u
                act.wait_ge(S["y_done"], i + 1)
                act.wait_ge(S["gate_copied"], i + 1)
                if not first:
                    act.wait_ge(S[f"scattered{u}"], 16 * t)
                for hf in range(2):
                    A_(yb[:, u, 512 * hf:512 * hf + 512], ps[5 + hf][:, :], ACT.Copy, scale=gatecol[:, u, :])\
                        .then_inc(S["y_copied"], 1)

            LAST = PAIRS // 2 - 1
            rows_copy(0, 0, True)
            silu(0, 0, True)
            rows_copy(0, 1, True)
            silu(0, 1, True)
            for t, first in ((1, True),):
                rows_copy(t, 0)
                rows_out(t - 1, 0, first)
                silu(t, 0)
                rows_copy(t, 1)
                rows_out(t - 1, 1, first)
                silu(t, 1)
            with act.Fori(2, PAIRS // 2) as t:
                rows_copy(t, 0)
                rows_out(t - 1, 0)
                silu(t, 0)
                rows_copy(t, 1)
                rows_out(t - 1, 1)
                silu(t, 1)
            rows_out(LAST, 0)
            rows_out(LAST, 1)
            act.wait_ge(S["np_ready"], 1)
            passes = act.value_load(npi[0:1, 0:1], min_val=1, max_val=MAXPASS)
            with act.If(passes > 1):
                with act.Fori(PAIRS // 2, passes * (PAIRS // 2)) as t:
                    for u in range(2):
                        rows_copy(t, u)
                        silu(t, u)
                        rows_out(t, u)
            for t in range(T):
                act.wait_ge(S["x3_ready"], t + 1)
                run(A_(sq3, x2[:, t, :], ACT.Square, accum_out=stat[:, 40 + t:41 + t]), "y3_ssq")
            for t in range(T):
                act.wait_ge(S["yout_ready"], t + 1)
                act.dma_start(A["o_y"][t, :, :], yout[:, t, :]).then_inc(S["y_out"], 16)
            act.wait_ge(S["y_out"], 16 * T)
            act.wait_ge(S["hf_out"], 16)

        @block.vector
        def _(dve):
            run = Own(dve, dve_own)
            tt, ts, stt = nc.vector.tensor_tensor, nc.vector.tensor_scalar, nc.vector.scalar_tensor_tensor
            tred = nc.vector.tensor_reduce

            def bc(v, axis, n):
                v = v.unsqueeze(axis)
                shape = list(v.shape)
                shape[axis] = n
                return v.broadcast_to(shape)

            dve.wait_ge(S["x_ssq"], T)
            run(ts(stat[:, 4:7], stat[:, 0:3], 1.0 / D, EPS, MUL, ADD), "x_ms")
            are, aim = vecs[:, V_ARE:V_ARE + NST], vecs[:, V_AIM:V_AIM + NST]
            d_ = lambda n: disc[:, n, :]
            dve.wait_ge(S["disc_exp"], 1)
            run(tt(d_(1), are, d_(0), MUL), "expin_ready")
            run(tt(d_(3), aim, d_(0), MUL))
            MAGIC = 12582912.0
            run(ts(d_(7), d_(3), float(1 / (2 * np.pi)), MAGIC, MUL, ADD))
            run(ts(d_(7), d_(7), MAGIC, None, SUB))
            c1 = 6.28125
            c2 = float(np.float32(2 * np.pi - c1))
            c3 = float(2 * np.pi - c1 - c2)
            run(stt(d_(3), d_(7), -c1, d_(3), MUL, ADD))
            run(stt(d_(3), d_(7), -c2, d_(3), MUL, ADD))
            run(stt(d_(4), d_(7), -c3, d_(3), MUL, ADD))
            PI = 3.1415925
            run(ts(d_(4), d_(4), PI, -PI, ALU.min, ALU.max), "ang_ready")
            dve.wait_ge(S["x_rstd"], 1)
            for t in range(T):
                run(ts(x_in[:, t, :], x_in[:, t, :], stat[:, 48 + t:49 + t], None, MUL), "xn_ready")
            dve.wait_ge(S["disc_sin"], 2)
            run(tt(d_(7), d_(6), d_(6), MUL))
            run(ts(d_(6), d_(7), -2.0, 1.0, MUL, ADD), "rotation_ready")
            run(tt(d_(8), d_(2), d_(6), MUL))
            run(ts(d_(8), d_(8), 1.0, None, SUB))
            run(tt(d_(9), d_(2), d_(5), MUL))
            run(tt(d_(10), are, are, MUL))
            run(tt(d_(11), aim, aim, MUL))
            run(tt(d_(10), d_(10), d_(11), ADD))
            run(nc.vector.reciprocal(d_(10), d_(10)))
            run(tt(d_(11), d_(8), are, MUL))
            run(tt(d_(12), d_(9), aim, MUL))
            run(tt(d_(11), d_(11), d_(12), ADD))
            run(tt(d_(11), d_(11), d_(10), MUL))
            run(tt(d_(12), d_(9), are, MUL))
            run(tt(d_(13), d_(8), aim, MUL))
            run(tt(d_(12), d_(12), d_(13), SUB))
            run(tt(d_(12), d_(12), d_(10), MUL))
            def mod_rows(m):
                o = multiplied(dve, ("ada", m))
                if m == 0:
                    dve.wait_ge(S["adab_in"], 16)
                else:
                    dve.wait_ge(S["adab_later_in"], 16 * m)
                run(tt(modrow[:, m, :], o[:, :], adab, ADD), frees=("ada", m))

            def scales(vec, norm, m):
                copied(dve, ("adaT", m))
                run(stt(scsh[:, vec], scsh[:, vec], 1.0, bc(vecs[:, norm:norm + KD], 2, NCOND), ADD, MUL), f"scales{vec}")

            def modulate(name, sc, sh):
                for k in range(KD):
                    o = multiplied(dve, (name, k))
                    dve.wait_ge(S[f"prompt_{name}"], k + 1)
                    smp = nT[:, k, SEQ:NTOK].rearrange("p (b f) -> p b f", f=FRAMES)
                    run(tt(smp, o[:, SEQ:NTOK].rearrange("p (b f) -> p b f", f=FRAMES),
                           bc(scsh[:, sc, k, 1:NCOND], 2, FRAMES), MUL))
                    run(tt(smp, smp, bc(scsh[:, sh, k, 1:NCOND], 2, FRAMES), ADD), frees=(name, k))

            mod_rows(0)
            scales(1, V_N1, 0)
            modulate("xT", 1, 0)
            fre, fim = bc(d_(11), 2, 32), bc(d_(12), 2, 32)
            dve.wait_ge(S["bb_in"], 16)
            run(tt(btmp[:, 0], bbraw[:, 0], fre, MUL))
            run(tt(btmp[:, 1], bbraw[:, 1], fim, MUL))
            run(tt(bbar[:, 0], btmp[:, 0], btmp[:, 1], SUB), "bbar_ready")
            run(tt(btmp[:, 0], bbraw[:, 1], fre, MUL))
            run(tt(btmp[:, 1], bbraw[:, 0], fim, MUL))
            run(tt(bbar[:, 1], btmp[:, 0], btmp[:, 1], ADD), "bbar_ready")
            dve.wait_ge(S["h0_in"], 16)
            for r in range(2):
                run(tt(h0[:, r], h0[:, r], bc(d_(2), 2, STREAMS), MUL))
            dve.wait_ge(S["ct_in"], 16)
            run(ts(ct[:, 1], ct[:, 1], -1.0, None, MUL))


            def split(v, high, low, ready):
                run(nc.vector.tensor_copy(high, v))
                run(tt(low, v, high, SUB), ready)

            def split_panel(n):
                key = split_keys[6 + n]
                panel_arrived(dve, key)
                high_place_free(dve, key)
                split(panel(key, PANEL, 1), panel_high(key, PANEL, 1), panel_low(key, PANEL, 1), "w_split")

            def lesser_parts(n):
                key = split_keys[n]
                dve.wait_ge(S["w_high"], n + 1)
                part = slice(0, PANEL // 4 if n else PANEL)
                run(tt(panel_low(key, PANEL, 1)[:, part], panel(key, PANEL, 1)[:, part], panel_high(key, PANEL, 1)[:, part], SUB),
                    "w_split")

            lesser_parts(0)
            dve.wait_ge(S["n1_high"], 1)
            multiplied(dve, ("u", 3))
            for k in range(0, KD, 2):
                run(tt(nTlow[:, k:k + 2, :], nT[:, k:k + 2, :], high1[:, k:k + 2, :], SUB), "n1_split")

            def state_tile(i):
                turns_ = rot[:, (i // 2) % 2, :, i % 2, :]
                m = [m4[:, n, :] for n in range(4)]
                twice = lambda v: bc(v, 1, 2)
                dve.wait_ge(S["rot_ready"], 2 * (i // 2 + 1))
                for r in range(2):
                    o = multiplied(dve, ("bu", i, r))[:, 0:NTOK]
                    run(tt(m4[:, r::2, :], turns_, twice(o), MUL), frees=("bu", i, r))
                run(tt(m[0], m[0], m[3], ADD))
                run(tt(m[1], m[1], m[2], SUB))
                run(tt(m4[:, 0:2, SEQ::FRAMES], m4[:, 0:2, SEQ::FRAMES], h0[:, :, i, :], ADD))
                dve.wait_ge(S["decay_ready"], i + 1)
                flat = lambda v: v.rearrange("p r t -> p (r t)")
                run(nc.vector.tensor_tensor_scan(flat(m4[:, 2:4, :]), flat(decay), flat(m4[:, 0:2, :]), 0.0, MUL, ADD))
                if i >= 2:
                    dve.wait_ge(S["y_read"], i - 1)
                    dve.wait_ge(S["h_copied"], 2 * (i - 1))
                h = hri[:, i % 2]
                run(tt(m4[:, 0:2, :], turns_, twice(m[2]), MUL))
                run(tt(h[:, ::-1, :], turns_, twice(m[3]), MUL))
                run(tt(h[:, 0, :], m[0], h[:, 0, :], SUB), "h_ready")
                run(tt(h[:, 1, :], m[1], h[:, 1, :], ADD), "h_ready")

            def skip(a):
                o = ps[4]
                dve.wait_ge(S["y_read"], 4 * (a + 1))
                run(stt(zT[:, a, :], uT[:, a, :], vecs[:, V_D + a:V_D + a + 1], o[:, 0:NTOK], MUL, ADD), frees=("y", a))

            for i in range(NST):
                state_tile(i)
                if i % 3 == 1 and i // 3 < 5:
                    lesser_parts(i // 3 + 1)
                if i % 4 == 1 and i > 4:
                    skip(i // 4 - 1)
            skip(3)
            dve.wait_ge(S["ret_in"], 16)
            rope = rc[:, R_ROPE:R_ROPE + 768].rearrange("p (t s d) -> p t s d", t=T, s=4)
            tmp = [rtm[:, n] for n in range(4)]
            for r in range(2):
                for t in range(T):
                    copied(dve, ("in", 1 + r, t))
                x1, x2_ = (qk[:, r].rearrange("p t (h s d) -> p t h s d", h=HEADS, s=2)[:, :, :, s, :] for s in range(2))
                cos, sin = (bc(rope[:, :, 2 * r + s, :], 2, HEADS) for s in range(2))
                run(tt(tmp[0], x1, cos, MUL))
                run(tt(tmp[1], x2_, sin, MUL))
                run(tt(tmp[2], x1, sin, MUL))
                run(tt(tmp[3], x2_, cos, MUL))
                run(tt(x1, tmp[0], tmp[1], SUB), "rope_done")
                run(tt(x2_, tmp[2], tmp[3], ADD), "rope_done")
            for c in range(4):
                copied(dve, ("glu", c))
                run(tt(oT[:, c, :], uT[:, c, :], zT[:, c, :], MUL), "oT_ready")

            def keys_and_scores(h):
                ks = slice(128 * h, 128 * h + 128)
                if h:
                    multiplied(dve, ("kvp", h - 1))
                    multiplied(dve, ("kvs", h - 1, 3))
                for t in range(2):
                    run(ts(kd[:, t, :], qk[:, 1, t, ks], rc[:, R_KD + HEADS * t + h:R_KD + HEADS * t + h + 1], None, MUL), "kd_ready")
                run(tt(kz, bc(qk[:, 1, 2, ks], 1, STREAMS),
                       bc(rc[:, R_ZM + STREAMS * h:R_ZM + STREAMS * h + STREAMS], 2, 128), MUL), "kz_ready")
                o = multiplied(dve, ("s", h))
                dve.wait_ge(S[f"mask_in{h % 2}"], 16 * (h // 2 + 1))
                if h >= 2:
                    multiplied(dve, ("oB", h - 2))
                run(tt(sT[:, h % 2, :], o[:, :], msk[:, h % 2, :], MUL), frees=("s", h))

            def retention(h):
                lg_ = float(np.log(1.0 - 2.0 ** (-5.0 - h)))
                o = multiplied(dve, ("kvp", h))
                if h:
                    dve.wait_ge(S["kv_out"], 16 * h)
                run(nc.vector.tensor_copy(kvo, o[:, 0:DV]), frees=("kvp", h))
                if h + 1 < HEADS:
                    keys_and_scores(h + 1)
                multiplied(dve, ("oB", h))
                for b2 in range(4):
                    o = multiplied(dve, ("kvs", h, b2))
                    st = s0[(2 * h + b2 // 2) % 3][:, 2 * (b2 % 2):2 * (b2 % 2) + 2, :]
                    run(stt(st, st, float(np.exp(lg_ * FRAMES)), o.rearrange("p (b d) -> p b d", b=2), MUL, ADD),
                        frees=("kvs", h, b2))
                dve.wait_ge(S["o_ssq"], T * (h + 1))
                run(ts(stat[:, 28:31], stat[:, 8 + T * h:11 + T * h], 1.0 / DV, EPS, MUL, ADD), "o_ms")
                dve.wait_ge(S["o_rstd"], h + 1)
                for t in range(T):
                    name = ("oA", h) if t < 2 else ("oB", h)
                    o = ps[turns[name][0]]
                    g = gg[:, t, DV * h:DV * h + DV]
                    run(stt(g, o[:, DV * (t % 2):DV * (t % 2) + DV], stat[:, 51 + t:52 + t], g, MUL, MUL), "og_ready")
                    if t:
                        run(ts(stat[:, 61:62], o[:, 0:1], 0.0, None, MUL), frees=name)

            dve.wait_ge(S["qx_zero"], 1)
            for h in range(HEADS):
                copied(dve, ("qT", h))
                qs = qT[:, h, SEQ:NTOK].rearrange("p (j r f) -> p j r f", r=2, f=FRAMES)
                xi = bc(rc[:, R_XI + FRAMES * h:R_XI + FRAMES * h + FRAMES], 1, 4)
                for r in range(2):
                    run(tt(qx[:, h, r::2, FRAMES * r:FRAMES * r + FRAMES], qs[:, :, r, :], xi, MUL), "qx_ready")
            keys_and_scores(0)
            mod_rows(1)
            retention(0)
            retention(1)
            mod_rows(2)
            retention(2)
            split_panel(0)
            retention(3)
            split_panel(1)
            scales(3, V_N2, 2)
            for r, n in enumerate((3, 3, 2)):
                dve.wait_ge(S[f"s0_out{r}"], 16 * n)
            dve.wait_ge(S["kv_out"], 16 * HEADS)
            split(oT, oThigh, oTlow, "oT_split")
            for n in range(2, 5):
                split_panel(n)
            multiplied(dve, ("in", 10, T - 1))
            for k in range(0, KD, 2):
                copied(dve, ("ogT", k))
                copied(dve, ("ogT", k + 1))
                split(ogT[:, k:k + 2, :], highT[:, k:k + 2, :], ogTlow[:, k:k + 2, :], "ogT_split")
            for hf in range(2):
                for t in range(T):
                    if (hf, t) == (0, 2):
                        split_panel(5)
                    o = multiplied(dve, ("ya", hf, t))
                    copied(dve, ("in", 7 + hf, t))
                    ga = gates[:, t, 512 * hf:512 * hf + 512]
                    run(tt(ga, ga, o[:, :], MUL), frees=("ya", hf, t))
            for hf in range(2):
                for t in range(T):
                    if t == 0:
                        split_panel(6 + hf)
                    o = multiplied(dve, ("yb", hf, t))
                    copied(dve, ("in", 9 + hf, t))
                    ga = gates[:, t, 512 * hf:512 * hf + 512]
                    gb = gates[:, t, 1024 + 512 * hf:1536 + 512 * hf]
                    run(tt(gb, gb, o[:, :], MUL), frees=("yb", hf, t))
                    run(tt(ga, ga, gb, ADD), "merged")
            for k in range(0, KD, 2):
                copied(dve, ("mT", k))
                copied(dve, ("mT", k + 1))
                split(nT[:, k:k + 2, :], highT[:, k:k + 2, :], nTlow[:, k:k + 2, :], "mT_split")
            split_panel(8)
            dve.wait_ge(S["x2_in"], 16 * T)
            for v in range(2):
                for hf in range(2):
                    copied(dve, ("g1", v, hf))
            for hf in range(2):
                for t in range(T):
                    o = multiplied(dve, ("wo", hf, t))
                    gb = gates[:, t, 1024 + 512 * hf:1536 + 512 * hf]
                    xs = x2[:, t, 512 * hf:512 * hf + 512]
                    run(tt(gb, gte[:, t // 2, 512 * hf:512 * hf + 512], o[:, :], MUL), frees=("wo", hf, t))
                    run(tt(xs, xs, gb, ADD), "x2_ready")
            dve.wait_ge(S["n2_ssq"], T)
            run(ts(stat[:, 32:35], stat[:, 24:27], 1.0 / D, EPS, MUL, ADD), "n2_ms")
            dve.wait_ge(S["n2_rstd"], 1)
            for t in range(T):
                run(ts(gg[:, t, :], x2[:, t, :], stat[:, 54 + t:55 + t], None, MUL), "xn2_ready")
            modulate("x2T", 3, 2)

            o = multiplied(dve, "logits")
            run(nc.vector.tensor_copy(lg.rearrange("p t e -> p (t e)"), o[:, 0:T * 36]), frees="logits")

            def first_largest(x, n, onehot, largest):
                w = tw[:, :, 0:n]
                run(tred(largest, x, AX.X, ALU.max))
                run(tt(w, x, bc(largest, 2, n), ALU.is_equal))
                run(tt(w, w, bc(const[:, C_REV:C_REV + n], 1, T), MUL))
                run(tred(nth, w, AX.X, ALU.max))
                run(tt(onehot, w, bc(nth, 2, n), ALU.is_equal))

            first_largest(lg[:, :, 0:GROUPS], GROUPS, goh, big[:, 0, :])
            ein = e_in[:, 0:12].rearrange("p (t g) -> p t g", t=T)
            run(tt(ein, lg[:, :, 0:GROUPS], bc(big[:, 0, :], 2, GROUPS), SUB), "e_in_ready")
            by_group = lambda v: v.rearrange("p t (g e) -> p t g e", g=GROUPS)
            run(tt(by_group(tg[:, 0]), by_group(lg[:, :, GROUPS:36]), bc(goh, 3, EXPERTS), MUL))
            run(tred(el, tg[:, 0].rearrange("p t (g e) -> p t e g", g=GROUPS), AX.X, ADD))
            first_largest(el, EXPERTS, eoh[:, 0], big[:, 1, :])
            run(stt(el2, eoh[:, 0], -1e30, el, MUL, ADD))
            first_largest(el2, EXPERTS, eoh[:, 1], big[:, 2, :])
            for k in range(2):
                run(tt(by_group(foh[:, k]), bc(goh, 3, EXPERTS), bc(eoh[:, k], 2, GROUPS), MUL))
            run(tt(sel, foh[:, 0], foh[:, 1], ADD), "sel_ready")
            run(tt(e_in[:, 12:15], big[:, 2, :], big[:, 1, :], SUB), "e_in_ready")
            kt6 = lambda v: v.rearrange("p k t -> p (k t)")
            foh6, tg6 = (v.rearrange("p k t e -> p (k t) e") for v in (foh, tg))
            for table, result in ((C_PAR, bslot), (C_PAIR, bpair)):
                run(tt(tg6, foh6, bc(const[:, table:table + NEXP], 1, 2 * T), MUL))
                run(tred(kt6(result), tg6, AX.X, ADD))
            dve.wait_ge(S["e_out_ready"], 1)
            run(tred(gw, e_out[:, 0:12].rearrange("p (t g) -> p t g", t=T), AX.X, ADD))
            run(stt(wk[:, 0, :], e_out[:, 12:15], 1.0, gw, ADD, MUL))
            run(nc.vector.reciprocal(wk[:, 0, :], wk[:, 0, :]))
            run(tt(wk[:, 1, :], wk[:, 0, :], e_out[:, 12:15], MUL))
            dve.wait_ge(S["rec_in"], 16)
            run(nc.vector.tensor_copy(rec[:, :, :, 2], wk))
            o = multiplied(dve, "rank")
            run(tt(tg.rearrange("p k t e -> p k (t e)"), foh.rearrange("p k t e -> p k (t e)"), bc(o[:, 0:T * NEXP], 1, 2), MUL),
                frees="rank")
            run(tred(kt6(rk), tg6, AX.X, ADD))
            run(tt(ps5.rearrange("p k t j -> p (k t) j"),
                   bc(kt6(rk), 2, 5), bc(const[:, C_PT:C_PT + 5], 1, 6), ALU.is_ge))
            run(tred(kt6(npass), ps5.rearrange("p k t j -> p (k t) j"), AX.X, ADD))
            run(stt(slot, npass, -float(CAP), rk, MUL, ADD))
            run(tt(slot, slot, bslot, ADD))
            run(stt(column, npass, float(PAIRS), bpair, MUL, ADD))
            rec6 = rec.rearrange("p k t w -> p (k t) w")

            def picks(first, n, onehot, values, ready):
                run(tt(onehot, bc(kt6(column), 2, n), bc(const[:, C_IOTA + first:C_IOTA + first + n], 1, 2 * T), ALU.is_equal))
                run(tt(values, bc(onehot, 3, META), bc(rec6, 2, n), MUL), ready)

            run(tt(soh, bc(kt6(slot), 2, 128), bc(const[:, C_IOTA:C_IOTA + 128], 1, 2 * T), ALU.is_equal))
            picks(0, PAIRS, coh, cval, "cval_ready")
            run(tred(npcol[:, 0:1], kt6(npass), AX.X, ALU.max))

            def read_records(name, first, n, ready):
                o = multiplied(dve, name)[:, 0:META * n].rearrange("p (c w) -> p c w", w=META)
                run(nc.vector.tensor_copy(metaf[:, first:first + n, 2], o[:, :, 2]))
                run(ts(metai[:, first:first + n, 0:2], o[:, :, 0:2], float(NO_ROW), None, ADD), ready)

            read_records("slots", 0, PAIRS, "records_ready")
            run(ts(nth[:, 0:1], npcol[:, 0:1], 1.0, None, MUL), frees="slots")
            dve.wait_ge(S["n2_out"], 16 * T)
            picks(PAIRS, LATER, coh2, cval2, "cval2_ready")
            read_records("slots2", PAIRS, LATER, "later_records")
            run(ts(nth[:, 0:1], npcol[:, 0:1], 1.0, None, MUL), frees="slots2")
            o = multiplied(dve, "np")
            run(tred(npcol[0:1, 1:2], o[0:1, 0:128], AX.X, ALU.max), frees="np")
            run(ts(npi[0:1, 0:1], npcol[0:1, 1:2], 1.0, None, ADD), "np_ready")
            passes = dve.value_load(npi[0:1, 0:1], min_val=1, max_val=MAXPASS)

            def pair(t, u, first=False):
                i = 2 * t + u
                dve.wait_ge(S["silu_ready"], i + 1)
                tt(hs[:, u, :], hs[:, u, :], ps[2 + u][:, FF:2 * FF], MUL).then_inc(S["hs_ready"], 1)
                dve.wait_ge(S["hTp_done"], i + 1)
                if not first:
                    dve.wait_ge(S["y_done"], i - 1)
                nc.vector.tensor_copy(hT[:, u].rearrange("p k s -> p (k s)"), ps[4][:, 0:FF]).then_inc(S["hT_ready"], 1)

            pair(0, 0, True)
            pair(0, 1, True)
            with dve.Fori(1, PAIRS // 2) as t:
                pair(t, 0)
                pair(t, 1)
            with dve.If(passes > 1):
                with dve.Fori(PAIRS // 2, passes * (PAIRS // 2)) as t:
                    pair(t, 0)
                    pair(t, 1)
            for v in range(2):
                for hf in range(2):
                    copied(dve, ("g2", v, hf))
            dve.wait_ge(S["fn_in"], 16)
            def mean_square(t):
                dve.wait_ge(S["y3_ssq"], t + 1)
                run(ts(stat[:, 44 + t:45 + t], stat[:, 40 + t:41 + t], 1.0 / D, EPS, MUL, ADD), "y3_ms")

            for t in range(T):
                dve.wait_ge(S[f"ys_in{t}"], 16)
                y = ys[:, t, 0, :]
                if t == T - 1:
                    dve.wait_ge(S["y_summed"], 1)
                else:
                    run(tt(y, y, ys[:, t, 1, :], ADD))
                run(tt(y, y, gte[:, t // 2, :], MUL))
                if t:
                    mean_square(t - 1)
                run(tt(x2[:, t, :], x2[:, t, :], y, ADD), "x3_ready")
            for t in range(T):
                if t == T - 1:
                    mean_square(t)
                dve.wait_ge(S["y3_rstd"], t + 1)
                run(stt(yout[:, t, :], x2[:, t, :], stat[:, 57 + t:58 + t], fnorm, MUL, MUL), "yout_ready")

        @block.gpsimd
        def _(pool):
            run = Own(pool, pool_own)
            tt = nc.gpsimd.tensor_tensor

            def bc(v, axis, n):
                v = v.unsqueeze(axis)
                shape = list(v.shape)
                shape[axis] = n
                return v.broadcast_to(shape)

            run(nc.gpsimd.memset(btp, 0.0), "zeros_ready")
            half = const[:, C_HALF:C_HALF + 3]
            pool.wait_ge(S["const_in"], 16)
            pool.wait_ge(S["x_ms"], 1)
            run(tt(stat[:, 48:51], stat[:, 4:7], half, ALU.pow), "x_rstd")
            pool.wait_ge(S["rotation_ready"], 1)
            pre, pim = pw[:, 0], pw[:, 1]
            cpy = nc.gpsimd.tensor_copy
            run(nc.gpsimd.memset(pre[:, :, 16:40], 1.0))
            run(nc.gpsimd.memset(pim[:, :, 16:40], 0.0))
            run(cpy(pre[:, :, 0], disc[:, 6, :]))
            run(cpy(pim[:, :, 0], disc[:, 5, :]))

            def doubled(o, n):
                cr, ci = pre[:, :, o + n - 1:o + n].broadcast_to([128, NST, n]), pim[:, :, o + n - 1:o + n].broadcast_to([128, NST, n])
                ar, ai = pre[:, :, o:o + n], pim[:, :, o:o + n]
                ta, tb = ptmp[:, 0, :, 0:n], ptmp[:, 1, :, 0:n]
                run(tt(ta, ar, cr, MUL))
                run(tt(tb, ai, ci, MUL))
                m = min(n, (16 if o == 0 else 15) - n)
                run(tt(pre[:, :, o + n:o + n + m], ta[:, :, 0:m], tb[:, :, 0:m], SUB))
                run(tt(ta, ar, ci, MUL))
                run(tt(tb, ai, cr, MUL))
                run(tt(pim[:, :, o + n:o + n + m], ta[:, :, 0:m], tb[:, :, 0:m], ADD))

            for n in (1, 2, 4, 8):
                doubled(0, n)
            run(cpy(pre[:, :, 17], pre[:, :, 15]))
            run(cpy(pim[:, :, 17], pim[:, :, 15]))
            for n in (1, 2, 4, 8):
                doubled(17, n)
            pool.wait_ge(S["silu_c"], 1)

            def lesser_parts(n):
                key, part = split_keys[n], slice(PANEL // 4, PANEL)
                pool.wait_ge(S["w_high"], n + 1)
                run(tt(panel_low(key, PANEL, 1)[:, part], panel(key, PANEL, 1)[:, part], panel_high(key, PANEL, 1)[:, part], SUB),
                    "w_split_rest")

            for a in range(NST // 2):
                if a in (2, 4, 5, 6):
                    lesser_parts({2: 1, 4: 2, 5: 3, 6: 4}[a])
                if a >= 2:
                    pool.wait_ge(S["h_ready"], 4 * (a - 1))
                tmp = rtmp.rearrange("p i (a b) -> p i a b", b=16)
                for i in range(2):
                    n = 2 * a + i
                    tv = [bc(pw[:, r, n, 16:40], 2, 16) for r in range(2)]
                    bv = [bc(pw[:, r, n, 0:16], 1, 24) for r in range(2)]
                    dst = [rot[:, a % 2, r, i, :].rearrange("p (a b) -> p a b", b=16) for r in range(2)]
                    for r, op in ((0, SUB), (1, ADD)):
                        run(tt(tmp[:, 0], tv[0], bv[r], MUL))
                        run(tt(tmp[:, 1], tv[1], bv[1 - r], MUL))
                        run(tt(dst[r], tmp[:, 0], tmp[:, 1], op), "rot_ready" if i else None)
            lesser_parts(5)
            copied(pool, ("ada", 0))
            pool.dma_start(adab, A["b_ada"][1, :, :]).then_inc(S["adab_later_in"], 16)
            copied(pool, ("y", 3))
            pool.wait_ge(S["h_copied"], 2 * NST)
            for h in range(2):
                pool.dma_start(msk[:, h, :], A["c_mask"][h, :, :]).then_inc(S[f"mask_in{h}"], 16)

            def states_in(n):
                pool.dma_start(s0[n % 3], A["s0"][n // 2, :, 4 * (n % 2):4 * (n % 2) + 4, :]).then_inc(S[f"s0_in{n % 3}"], 16)

            states_in(0)
            states_in(1)
            pool.wait_ge(S["hf_out"], 16)
            states_in(2)
            pool.wait_ge(S["rope_done"], 4)
            run(nc.gpsimd.memset(qx, 0.0), "qx_zero")
            pool.wait_ge(S["adab_later_in"], 16)
            copied(pool, ("ada", 1))
            pool.dma_start(adab, A["b_ada"][2, :, :]).then_inc(S["adab_later_in"], 16)
            for h in range(HEADS):
                copied(pool, ("kvp", h))
                if h + 2 < HEADS:
                    copied(pool, ("s", h))
                    pool.dma_start(msk[:, h % 2, :], A["c_mask"][h + 2, :, :]).then_inc(S[f"mask_in{h % 2}"], 16)
                pool.dma_start(A["o_retp"][h, :, :], kvo).then_inc(S["kv_out"], 16)
                for n in (2 * h, 2 * h + 1):
                    copied(pool, ("kvs", h, 2 * (n % 2) + 1))
                    pool.dma_start(A["o_rets"][h, :, 4 * (n % 2):4 * (n % 2) + 4, :], s0[n % 3]).then_inc(S[f"s0_out{n % 3}"], 16)
                pool.wait_ge(S["o_ms"], h + 1)
                if h:
                    pool.wait_ge(S["og_ready"], T * h)
                run(tt(stat[:, 51:54], stat[:, 28:31], half, ALU.pow), "o_rstd")
                for n in (2 * h + 3, 2 * h + 4):
                    if n < 2 * HEADS:
                        pool.wait_ge(S[f"s0_out{n % 3}"], 16 * (n // 3))
                        states_in(n)
            for r, n in enumerate((3, 3, 2)):
                pool.wait_ge(S[f"s0_out{r}"], 16 * n)
            pool.wait_ge(S["kv_out"], 16 * HEADS)
            pool.wait_ge(S["og_ready"], T * HEADS)
            for t in range(T):
                pool.dma_start(x2[:, t, :], A["x"][t, :, :]).then_inc(S["x2_in"], 16)
            pool.dma_start(spread, A["c_spread"]).then_inc(S["spread_in"], 16)
            pool.wait_ge(S["n2_ms"], 1)
            run(tt(stat[:, 54:57], stat[:, 32:35], half, ALU.pow), "n2_rstd")
            pool.wait_ge(S["x2_ready"], 6)
            run(nc.gpsimd.memset(xg, 0.0), "xg_zero")
            pool.wait_ge(S["records_ready"], 1)
            ind = bass.IndirectOffsetOnAxis
            pool.wait_ge(S["n2_out"], 16 * T)

            def gather(t, u, first=False):
                i = 2 * t + u
                if not first:
                    pool.wait_ge(S["tr_done"], i - 1)
                pool.wait_ge(S["records_ready"], 1)
                nc.gpsimd.tensor_copy(gidx[:, u, :], metai[:, bass.ds(i, 1), 0]).then_inc(S["gidx_copied"], 1)
                pool.wait_ge(S["gidx_copied"], i + 1)
                pool.nop(nofuse=True)
                nc.gpsimd.indirect_dma_start(out=xg[:, u, :], out_offset=None, in_=n2_d,
                                             in_offset=ind(ap=gidx[:, u, 0:1], axis=0),
                                             bounds_check=NTOK - 1, oob_is_err=False).then_inc(S[f"gathered{u}"], 16)

            def scatter(t, u, first=False):
                i = 2 * t + u
                if not first:
                    pool.wait_ge(S[f"scattered{u}"], 16 * t)
                pool.wait_ge(S["records_ready"], 1)
                nc.gpsimd.tensor_copy(sidx[:, u, :], metai[:, bass.ds(i, 1), 1]).then_inc(S["sidx_copied"], 1)
                pool.wait_ge(S["sidx_copied"], i + 1)
                pool.wait_ge(S["y_copied"], 2 * i + 2)
                pool.nop(nofuse=True)
                nc.gpsimd.indirect_dma_start(out=y_d, out_offset=ind(ap=sidx[:, u, 0:1], axis=0),
                                             in_=yb[:, u, :], in_offset=None,
                                             bounds_check=2 * NTOK - 1, oob_is_err=False).then_inc(S[f"scattered{u}"], 16)

            gather(0, 0, True)
            gather(0, 1, True)
            gather(1, 0)
            gather(1, 1)
            pool.dma_start(fnorm, A["final_norm"].partition_broadcast(128)).then_inc(S["fn_in"], 16)
            scatter(0, 0, True)
            gather(2, 0)
            scatter(0, 1, True)
            gather(2, 1)
            scatter(1, 0)
            with pool.Fori(2, PAIRS // 2 - 1) as t:
                gather(t + 1, 0)
                scatter(t - 1, 1)
                gather(t + 1, 1)
                scatter(t, 0)
            scatter(PAIRS // 2 - 2, 1)
            scatter(PAIRS // 2 - 1, 0)
            scatter(PAIRS // 2 - 1, 1)
            for u in range(2):
                pool.wait_ge(S[f"scattered{u}"], 16 * (PAIRS // 2))
            pool.wait_ge(S["np_ready"], 1)
            passes = pool.value_load(npi[0:1, 0:1], min_val=1, max_val=MAXPASS)
            with pool.If(passes > 1):
                with pool.Fori(PAIRS // 2, passes * (PAIRS // 2)) as t:
                    for u in range(2):
                        gather(t, u)
                        scatter(t, u)
                for u in range(2):
                    pool.wait_ge(S[f"scattered{u}"], 16 * (PAIRS // 2) * passes)
            run(nc.gpsimd.memset(gidx, 0), "rows_out")
            pool.wait_ge(S[f"ys_in{T - 1}"], 16)
            run(tt(ys[:, T - 1, 0, :], ys[:, T - 1, 0, :], ys[:, T - 1, 1, :], ADD), "y_summed")
            for t in range(T):
                pool.wait_ge(S["y3_ms"], t + 1)
                run(tt(stat[:, 57 + t:58 + t], stat[:, 44 + t:45 + t], half[:, 0:1], ALU.pow), "y3_rstd")


def kernel(**inputs):
    import concourse.bacc as bacc
    from concourse.bass_utils import run_bass_kernel_spmd as run

    g = {k: np.asarray(v) for k, v in inputs.items()}
    C = np.ascontiguousarray
    l = 0
    G, P, J = 32, 64, 16

    def rows(w, kt, n):
        return w.reshape(kt, 128, n).transpose(1, 0, 2).reshape(128, kt * n)

    def panels(w, kt, width):
        n = w.shape[1] // width
        return C(w.reshape(kt, 128, n, width).transpose(2, 1, 0, 3).reshape(n, 128, kt * width))

    arrays = {}
    arrays["x"] = C(np.concatenate([g["x_prompt"].reshape(-1, D), g["x_sample"].reshape(-1, D)]).reshape(T, 128, D))
    cond = np.zeros((32, D), np.float32)
    cond[0] = g["c_prompt"][0]
    cond[1:NCOND] = g["c_sample"]
    arrays["condT"] = C(cond.T.reshape(KD, 128, 32).transpose(1, 0, 2).reshape(128, -1))
    arrays["p_ada"] = C(g["w_ada"][l].reshape(4, 2, 128, 3, 2048).transpose(3, 0, 2, 1, 4).reshape(12, 128, -1))
    arrays["p_in"] = panels(g["w_in"][l], KD, 512)
    arrays["p_glu"] = panels(g["s5_w_glu"][l], 4, 512)
    arrays["p_s5"] = panels(g["w_s5_out"][l], 4, 1024)
    arrays["p_ret"] = panels(g["w_ret_out"][l], KD, 512)
    arrays["p_out"] = panels(g["w_out"][l], KD, 512)
    arrays["b_ada"] = C(np.repeat(g["b_ada"][l].reshape(3, 4, 1, 512), 32, 2).reshape(3, 128, 512))
    by_state = lambda a: a.reshape(NST, 128).T
    by_chan = lambda a: a.reshape(-1, 128).T
    v = np.zeros((128, V_N), np.float32)
    v[:, V_DT:V_DT + NST] = by_state(np.repeat(g["s5_log_dt"][l][:, None], P, 1))
    v[:, V_ARE:V_ARE + NST] = by_state(g["s5_a_re"][l])
    v[:, V_AIM:V_AIM + NST] = by_state(g["s5_a_im"][l])
    v[:, V_N1:V_N1 + KD] = by_chan(g["norm1"][l])
    v[:, V_N2:V_N2 + KD] = by_chan(g["norm2"][l])
    v[:, V_D:V_D + 4] = by_chan(g["s5_d"][l])
    v[:, V_BG:V_BG + 4] = by_chan(g["s5_b_glu"][l])
    v[0:GROUPS, V_BR] = g["b_rg"][l]
    v[GROUPS:36, V_BR] = g["b_re"][l].reshape(-1)
    arrays["vecs"] = v
    bb = np.zeros((128, 2, NST, 32), np.float32)
    ct = np.zeros((128, 2, NST, 32), np.float32)
    for r, (bn, cn) in enumerate((("s5_b_re", "s5_c_re"), ("s5_b_im", "s5_c_im"))):
        b = g[bn][l].reshape(NST, 2, P, J)
        c = g[cn][l].reshape(NST, 2, J, P)
        for par in range(2):
            bb[P * par:P * par + P, r, :, J * par:J * par + J] = b[:, par].transpose(1, 0, 2)
            ct[P * par:P * par + P, r, :, J * par:J * par + J] = c[:, par].transpose(2, 0, 1)
    arrays["bb"] = bb.reshape(128, -1)
    arrays["ct"] = ct.reshape(128, -1)
    h0 = np.stack([g[n][l].reshape(STREAMS, NST, 128).transpose(2, 1, 0) for n in ("state_s5_re", "state_s5_im")], 1)
    arrays["h0"] = C(h0.reshape(128, -1))
    arrays["s0"] = C(g["state_ret"][l].transpose(1, 2, 0, 3))
    wr = np.concatenate([g["w_rg"][l], g["w_re"][l].transpose(1, 0, 2).reshape(D, NEXP)], 1)
    arrays["w_router"] = C(rows(wr, KD, 36))
    w13 = np.concatenate([g["w1"][l].reshape(NEXP, KD, 128, FF), g["w3"][l].reshape(NEXP, KD, 128, FF)], 3)
    w13 = w13.transpose(0, 2, 1, 3).reshape(NEXP, 128, -1)
    w2 = g["w2"][l].reshape(NEXP, 2, 128, D).transpose(0, 2, 1, 3).reshape(NEXP, 128, -1)
    arrays["p_up"] = C(w13.reshape(PAIRS, 2, 128, -1).transpose(0, 2, 1, 3))
    arrays["p_down"] = C(w2.reshape(PAIRS, 2, 128, -1).transpose(0, 2, 1, 3))
    arrays["final_norm"] = C(g["final_norm"].reshape(-1))
    arrays.update({k: C(a) for k, a in shape_constants().items()})

    nc = bacc.Bacc("TRN2", target_bir_lowering=False, num_devices=1)
    A = {}
    for name, a in arrays.items():
        A[name] = nc.dram_tensor(f"in_{name}", a.shape, mybir.dt.from_np(a.dtype), kind="ExternalInput").ap()
    outs = {"o_y": (T, 128, D), "o_s5": (128, 2 * NST * NCOND), "o_retp": (HEADS, DK, DV), "o_rets": (HEADS, DK, STREAMS, DV)}
    for name, shape in outs.items():
        A[name] = nc.dram_tensor(f"out_{name}", shape, mybir.dt.float32, kind="ExternalOutput").ap()
    build(nc, A)
    r = run(nc, [{f"in_{k}": a for k, a in arrays.items()}], core_ids=[0]).results[0]
    y = r["out_o_y"].reshape(NTOK, D)
    s5 = r["out_o_s5"].reshape(128, 2, NST, NCOND).transpose(1, 3, 2, 0).reshape(2, NCOND, G, P)
    rp = r["out_o_retp"].reshape(1, 1, HEADS, DK, DV)
    rs = r["out_o_rets"].transpose(2, 0, 1, 3).reshape(1, STREAMS, HEADS, DK, DV)
    return (C(y[:SEQ].reshape(1, SEQ, D)), C(y[SEQ:].reshape(STREAMS, FRAMES, D)),
            C(s5[0, 0:1][None]), C(s5[1, 0:1][None]), C(rp), C(s5[0, 1:][None]), C(s5[1, 1:][None]), C(rs))
```
